# Optimizing a Trainium2 kernel written in Bass

```python
import jax, jax.numpy as jnp
from jax import lax
import numpy as np
import math
import jax
import jax.numpy as jnp

D_MODEL = 1024
BATCH = 1
SEQ = 256
DEPTH = 1

CHUNK = 64

D_POOL = D_MODEL // 2
POOL_WINDOWS = (2, 4, 8, 16)
POOL_GROUPS = len(POOL_WINDOWS)
POOL_GROUP_DIM = D_POOL // POOL_GROUPS

D_CONV = D_MODEL // 2
CONV_WIDTH = 3

D_IN = D_POOL + 3 * D_CONV + 2 * D_MODEL

N_KEYS = 128
N_EXPERTS = N_KEYS * N_KEYS
PEER_HEADS = 8
PEER_QUERY_DIM = 256
PEER_HALF = PEER_QUERY_DIM // 2
PEER_TOPK = 16
PEER_TOKEN_BLOCK = 128

RMS_EPS = 1e-6


def rmsnorm(x, g):
    xf = x.astype(jnp.float32)
    y = xf * lax.rsqrt(jnp.mean(xf * xf, axis=-1, keepdims=True) + RMS_EPS)
    return (y * g.astype(jnp.float32)).astype(x.dtype)

def pool_mixer(u, group_w, scale):
    S_ = u.shape[1]
    uf = u.astype(jnp.float32)
    csum = jnp.cumsum(uf, axis=1)
    pos = jnp.arange(S_)
    outs = []
    for g, w in enumerate(POOL_WINDOWS):
        sl = slice(g * POOL_GROUP_DIM, (g + 1) * POOL_GROUP_DIM)
        c = csum[:, :, sl]
        c_shift = jnp.pad(c[:, :S_ - w, :], ((0, 0), (w, 0), (0, 0)))
        cnt = jnp.minimum(pos + 1, w).astype(jnp.float32)[None, :, None]
        outs.append((c - c_shift) / cnt - uf[:, :, sl])
    p = jnp.stack(outs, axis=2).astype(u.dtype)
    p = jnp.einsum('bsgc,gcd->bsgd', p, group_w)
    return p.reshape(u.shape) * scale

def short_conv_mixer(c_gate, b_gate, v, conv_w):
    S_ = v.shape[1]
    u = c_gate * v
    up = jnp.pad(u, ((0, 0), (CONV_WIDTH - 1, 0), (0, 0)))
    y = up[:, 0:S_, :] * conv_w[0]
    for k in range(1, CONV_WIDTH):
        y = y + up[:, k:k + S_, :] * conv_w[k]
    return b_gate * y

def peer_ffn(h, w_q, sub_keys, expert_u, expert_v):
    B_, S_, D_ = h.shape
    hb_all = h.reshape(B_ * S_ // PEER_TOKEN_BLOCK, PEER_TOKEN_BLOCK, D_)

    def block(hb):
        q = (hb @ w_q).reshape(PEER_TOKEN_BLOCK, PEER_HEADS, 2, PEER_HALF)
        s = jnp.einsum('thpc,hpkc->thpk', q, sub_keys).astype(jnp.float32)
        top_s, top_i = lax.top_k(s, PEER_TOPK)
        cand_s = top_s[:, :, 0, :, None] + top_s[:, :, 1, None, :]
        cand_i = top_i[:, :, 0, :, None] * N_KEYS + top_i[:, :, 1, None, :]
        cand_s = cand_s.reshape(PEER_TOKEN_BLOCK, PEER_HEADS, PEER_TOPK * PEER_TOPK)
        cand_i = cand_i.reshape(PEER_TOKEN_BLOCK, PEER_HEADS, PEER_TOPK * PEER_TOPK)
        fin_s, fin_pos = lax.top_k(cand_s, PEER_TOPK)
        idx = jnp.take_along_axis(cand_i, fin_pos, axis=-1)
        gates = jax.nn.softmax(fin_s, axis=-1)
        u = expert_u[idx]
        act = jax.nn.gelu(jnp.einsum('thkd,td->thk', u, hb).astype(jnp.float32), approximate=False)
        wts = (gates * act).astype(hb.dtype)
        return jnp.einsum('thk,thkd->td', wts, expert_v[idx])

    out = lax.map(block, hb_all)
    return out.reshape(B_, S_, D_)

def first_inputs(seed: int = 0) -> dict:
    key = jax.random.key(seed)
    ks = jax.random.split(key, 16)
    f32 = jnp.float32
    nrm = lambda k, shape, s: jax.random.normal(k, shape, f32) * s
    L = DEPTH
    return {
        "x": nrm(ks[0], (BATCH, SEQ, D_MODEL), 1.0),
        "g_mix": 1.0 + nrm(ks[1], (L, D_MODEL), 0.02),
        "w_in": nrm(ks[2], (L, D_MODEL, D_IN), D_MODEL ** -0.5),
        "pool_group_w": nrm(ks[3], (L, POOL_GROUPS, POOL_GROUP_DIM, POOL_GROUP_DIM), POOL_GROUP_DIM ** -0.5),
        "pool_scale": 1.0 + nrm(ks[4], (L, D_POOL), 0.02),
        "conv_w": nrm(ks[5], (L, CONV_WIDTH, D_CONV), CONV_WIDTH ** -0.5),
        "w_branch_pool": nrm(ks[6], (L, D_POOL, D_MODEL), D_POOL ** -0.5),
        "w_branch_conv": nrm(ks[7], (L, D_CONV, D_MODEL), D_CONV ** -0.5),
        "w_out": nrm(ks[8], (L, D_MODEL, D_MODEL), D_MODEL ** -0.5),
        "g_ffn": 1.0 + nrm(ks[9], (L, D_MODEL), 0.02),
        "w_q": nrm(ks[10], (L, D_MODEL, PEER_HEADS * PEER_QUERY_DIM), D_MODEL ** -0.5),
        "sub_keys": nrm(ks[11], (L, PEER_HEADS, 2, N_KEYS, PEER_HALF), PEER_HALF ** -0.5),
        "expert_u": nrm(ks[12], (L, N_EXPERTS, D_MODEL), D_MODEL ** -0.5),
        "expert_v": nrm(ks[13], (L, N_EXPERTS, D_MODEL), PEER_HEADS ** -0.5),
        "g_final": 1.0 + nrm(ks[14], (D_MODEL,), 0.02),
    }

def first_block(x, g_mix, w_in, pool_group_w, pool_scale, conv_w, w_branch_pool, w_branch_conv,
              w_out, g_ffn, w_q, sub_keys, expert_u, expert_v, g_final):
    for l in range(DEPTH):
        h = rmsnorm(x, g_mix[l])
        z = h @ w_in[l]
        o1 = D_POOL
        o2 = o1 + D_CONV
        o3 = o2 + D_CONV
        o4 = o3 + D_CONV
        o5 = o4 + D_MODEL
        z_pool, z_c, z_b, z_v = z[..., :o1], z[..., o1:o2], z[..., o2:o3], z[..., o3:o4]
        gate_a, gate_b = z[..., o4:o5], z[..., o5:]
        a = pool_mixer(z_pool, pool_group_w[l], pool_scale[l]) @ w_branch_pool[l]
        b = short_conv_mixer(z_c, z_b, z_v, conv_w[l]) @ w_branch_conv[l]
        m = jax.nn.sigmoid(gate_a) * a + jax.nn.sigmoid(gate_b) * b
        x = x + m @ w_out[l]
        h2 = rmsnorm(x, g_ffn[l])
        x = x + peer_ffn(h2, w_q[l], sub_keys[l], expert_u[l], expert_v[l])
    return rmsnorm(x, g_final)


DEPTH_2 = 2

N_A_LAYERS = DEPTH_2 // 2
N_B_LAYERS = DEPTH_2 - N_A_LAYERS
MEM_LEN = 256
MEM_HEADS = 4
MEM_HEAD_DIM = 64
MEM_W = MEM_HEADS * MEM_HEAD_DIM
MIX_W = D_MODEL
MAIN_W = MIX_W - MEM_W
GLA_HEADS = 4
GLA_DV = MAIN_W // GLA_HEADS
GLA_DK = GLA_DV // 2
GLA_RANK = 16
GLA_GATE_NORM = 16.0
GLA_CHUNK = 16
NSA_HEADS = 12
NSA_GROUPS = 4
NSA_HEAD_DIM = MAIN_W // NSA_HEADS
NSA_REP = NSA_HEADS // NSA_GROUPS
CMP_BLOCK = 32
CMP_STRIDE = 16
CMP_HIDDEN = 128
SEL_BLOCK = 64
SEL_TOPK = 16
WINDOW = 512
Q_BLOCK = 64
REL_BUCKETS = 32
REL_MAX_DIST = 128
FFN_DIM = 2816
EPS = 1e-6
GLA_SIZES = (GLA_HEADS * GLA_DK, GLA_HEADS * GLA_DK, GLA_HEADS * GLA_DV, GLA_HEADS * GLA_DV, GLA_RANK, MEM_W)
GLA_IN = sum(GLA_SIZES)
NSA_SIZES = (NSA_HEADS * NSA_HEAD_DIM, NSA_HEADS * 3, MEM_W)
NSA_IN = sum(NSA_SIZES)
SHARED_KV_W = 6 * NSA_GROUPS * NSA_HEAD_DIM


def rmsnorm_2(x, g):
    xf = x.astype(jnp.float32)
    y = xf * lax.rsqrt(jnp.mean(xf * xf, axis=-1, keepdims=True) + EPS)
    return (y * g.astype(jnp.float32)).astype(x.dtype)

def split_cols(x, sizes):
    out = []
    start = 0
    for n in sizes:
        out.append(x[..., start:start + n])
        start += n
    return out

def rel_bucket(dist):
    dist = jnp.maximum(dist, 0)
    max_exact = REL_BUCKETS // 2
    large = max_exact + (jnp.log(jnp.maximum(dist, 1).astype(jnp.float32) / max_exact)
                         / math.log(REL_MAX_DIST / max_exact) * (REL_BUCKETS - max_exact)).astype(jnp.int32)
    large = jnp.minimum(large, REL_BUCKETS - 1)
    return jnp.where(dist < max_exact, dist, large)

def masked_softmax(s, mask):
    s = jnp.where(mask, s.astype(jnp.float32), -1e30)
    m = jnp.max(s, axis=-1, keepdims=True)
    p = jnp.where(mask, jnp.exp(s - m), 0.0)
    return p / jnp.maximum(jnp.sum(p, axis=-1, keepdims=True), 1e-30)

def gla_mixer(q, k, v, log_a, g_out, out_norm):
    dtype = v.dtype
    B, S = q.shape[0], q.shape[1]
    C = GLA_CHUNK
    N = S // C

    def chunked(t):
        return t.reshape(B, N, C, GLA_HEADS, t.shape[-1]).transpose(0, 3, 1, 2, 4).astype(jnp.float32)

    qc = chunked(q) * GLA_DK ** -0.5
    kc = chunked(k)
    vc = chunked(v)
    b = lax.cumsum(chunked(log_a), axis=3)
    causal = jnp.tril(jnp.ones((C, C), dtype=bool))
    diff = b[..., :, None, :] - b[..., None, :, :]
    decay = jnp.exp(jnp.where(causal[:, :, None], diff, -jnp.inf))
    attn = jnp.einsum('bhnid,bhnjd,bhnijd->bhnij', qc, kc, decay)
    o_intra = jnp.einsum('bhnij,bhnjv->bhniv', attn, vc)
    b_last = b[..., -1:, :]
    q_in = qc * jnp.exp(b)
    k_out = kc * jnp.exp(b_last - b)
    a_last = jnp.exp(b_last[..., 0, :])

    def step(state, inp):
        qi, ki, vi, ai = inp
        o = jnp.einsum('bhcd,bhdv->bhcv', qi, state)
        state = ai[..., None] * state + jnp.einsum('bhcd,bhcv->bhdv', ki, vi)
        return state, o

    xs = (jnp.moveaxis(q_in, 2, 0), jnp.moveaxis(k_out, 2, 0), jnp.moveaxis(vc, 2, 0), jnp.moveaxis(a_last, 2, 0))
    state0 = jnp.zeros((B, GLA_HEADS, GLA_DK, GLA_DV), jnp.float32)
    _, o_inter = lax.scan(step, state0, xs)
    o = o_intra + jnp.moveaxis(o_inter, 0, 2)
    o = o.transpose(0, 2, 3, 1, 4).reshape(B, S, GLA_HEADS, GLA_DV)
    o = rmsnorm_2(o, out_norm) * jax.nn.silu(g_out.astype(jnp.float32))
    return o.reshape(B, S, GLA_HEADS * GLA_DV).astype(dtype)

def mem_attention(q, mem_kv):
    B, S = q.shape[0], q.shape[1]
    M = mem_kv.shape[1]
    k, v = split_cols(mem_kv, (MEM_W, MEM_W))
    qh = q.reshape(B, S, MEM_HEADS, MEM_HEAD_DIM)
    kh = k.reshape(B, M, MEM_HEADS, MEM_HEAD_DIM)
    vh = v.reshape(B, M, MEM_HEADS, MEM_HEAD_DIM)
    s = jnp.einsum('bshd,bmhd->bhsm', qh, kh).astype(jnp.float32) * MEM_HEAD_DIM ** -0.5
    p = jax.nn.softmax(s, axis=-1)
    o = jnp.einsum('bhsm,bmhd->bshd', p, vh.astype(jnp.float32))
    return o.reshape(B, S, MEM_W).astype(q.dtype)

def shared_kv(h, kv_norm, w_kv, cmp_pos, cmp_w1, cmp_b1, cmp_w2, cmp_b2):
    B, S = h.shape[0], h.shape[1]
    G, Dh = NSA_GROUPS, NSA_HEAD_DIM
    kv = (rmsnorm_2(h, kv_norm) @ w_kv).reshape(B, S, 6, G, Dh).transpose(2, 0, 3, 1, 4)
    NC = (S - CMP_BLOCK) // CMP_STRIDE + 1
    win = jnp.arange(NC)[:, None] * CMP_STRIDE + jnp.arange(CMP_BLOCK)[None, :]

    def compress(t, j):
        blocks = t[:, :, win] + cmp_pos[j]
        flat = blocks.reshape(B, G, NC, CMP_BLOCK * Dh)
        return jax.nn.silu(flat @ cmp_w1[j] + cmp_b1[j]) @ cmp_w2[j] + cmp_b2[j]

    kc = compress(kv[0], 0)
    vc = compress(kv[1], 1)
    return (kc, vc, kv[2], kv[3], kv[4], kv[5])

def nsa_mixer(q, gates, shared, rel_bias):
    kc, vc, ks, vs, kw, vw = shared
    B, S = q.shape[0], q.shape[1]
    G, R, Dh = NSA_GROUPS, NSA_REP, NSA_HEAD_DIM
    NC = kc.shape[2]
    NSB = S // SEL_BLOCK
    n_sel = min(SEL_TOPK, NSB)
    qg = (q * Dh ** -0.5).reshape(B, S, G, R, Dh).transpose(0, 2, 3, 1, 4)
    gg = gates.reshape(B, S, G, R, 3).transpose(0, 2, 3, 1, 4)
    kb = ks.reshape(B, G, NSB, SEL_BLOCK, Dh)
    vb = vs.reshape(B, G, NSB, SEL_BLOCK, Dh)
    kw_p = jnp.pad(kw, ((0, 0), (0, 0), (WINDOW, 0), (0, 0)))
    vw_p = jnp.pad(vw, ((0, 0), (0, 0), (WINDOW, 0), (0, 0)))
    cmp_start = jnp.arange(NC) * CMP_STRIDE
    cmp_end = cmp_start + CMP_BLOCK - 1
    sel_idx = jnp.arange(NSB)
    sel_start = sel_idx * SEL_BLOCK
    overlap = ((cmp_start[:, None] < sel_start[None, :] + SEL_BLOCK)
               & (cmp_end[:, None] >= sel_start[None, :])).astype(jnp.float32)
    tbl = rel_bias.astype(jnp.float32).reshape(REL_BUCKETS, G, R)
    g_idx = jnp.arange(G)[None, :, None, None]

    def common_bias(dist):
        return tbl[rel_bucket(dist)].transpose(2, 3, 0, 1)

    def group_bias(dist):
        return jnp.moveaxis(tbl[rel_bucket(dist), g_idx], -1, 2)

    def block(c):
        t0 = c * Q_BLOCK
        t = t0 + jnp.arange(Q_BLOCK)
        qb = lax.dynamic_slice_in_dim(qg, t0, Q_BLOCK, axis=3)
        gb = lax.dynamic_slice_in_dim(gg, t0, Q_BLOCK, axis=3)
        d_c = t[:, None] - cmp_end[None, :]
        s_c = jnp.einsum('bgrqd,bgkd->bgrqk', qb, kc).astype(jnp.float32) + common_bias(d_c)
        p_c = masked_softmax(s_c, d_c >= 0)
        o_c = jnp.einsum('bgrqk,bgkd->bgrqd', p_c, vc.astype(jnp.float32))
        imp = jnp.einsum('bgrqk,kj->bgqj', p_c, overlap)
        cur = (t // SEL_BLOCK)[:, None]
        jj = sel_idx[None, :]
        forced = (jj == 0) | (jj == cur) | (jj == cur - 1)
        score = jnp.where(forced, 1e4, jnp.where(jj <= cur, imp, -1.0))
        _, idx = lax.top_k(score, n_sel)
        gather = jax.vmap(jax.vmap(lambda blk, ix: blk[ix]))
        k_sel = gather(kb, idx).reshape(B, G, Q_BLOCK, n_sel * SEL_BLOCK, Dh)
        v_sel = gather(vb, idx).reshape(B, G, Q_BLOCK, n_sel * SEL_BLOCK, Dh)
        pos = (idx[..., None] * SEL_BLOCK + jnp.arange(SEL_BLOCK)).reshape(B, G, Q_BLOCK, n_sel * SEL_BLOCK)
        d_s = t[None, None, :, None] - pos
        s_s = jnp.einsum('bgrqd,bgqkd->bgrqk', qb, k_sel).astype(jnp.float32) + group_bias(d_s)
        p_s = masked_softmax(s_s, (d_s >= 0)[:, :, None])
        o_s = jnp.einsum('bgrqk,bgqkd->bgrqd', p_s, v_sel.astype(jnp.float32))
        kwb = lax.dynamic_slice_in_dim(kw_p, t0, WINDOW + Q_BLOCK, axis=2)
        vwb = lax.dynamic_slice_in_dim(vw_p, t0, WINDOW + Q_BLOCK, axis=2)
        s_pos = t0 - WINDOW + jnp.arange(WINDOW + Q_BLOCK)
        d_w = t[:, None] - s_pos[None, :]
        mask_w = (d_w >= 0) & (d_w < WINDOW) & (s_pos[None, :] >= 0)
        s_w = jnp.einsum('bgrqd,bgkd->bgrqk', qb, kwb).astype(jnp.float32) + common_bias(d_w)
        p_w = masked_softmax(s_w, mask_w)
        o_w = jnp.einsum('bgrqk,bgkd->bgrqd', p_w, vwb.astype(jnp.float32))
        o = gb[..., 0:1] * o_c + gb[..., 1:2] * o_s + gb[..., 2:3] * o_w
        return o.astype(q.dtype)

    out = lax.map(block, jnp.arange(S // Q_BLOCK))
    return out.transpose(1, 0, 4, 2, 3, 5).reshape(B, S, NSA_HEADS * Dh)

def conv_ffn(x, w_up, conv_w, conv_b, w_down):
    S = x.shape[1]
    u = x @ w_up
    u_pad = jnp.pad(u, ((0, 0), (CONV_WIDTH - 1, 0), (0, 0)))
    hc = conv_b
    for j in range(CONV_WIDTH):
        hc = hc + conv_w[j] * u_pad[:, j:j + S]
    a, b = split_cols(hc, (FFN_DIM, FFN_DIM))
    return (jax.nn.silu(a) * b) @ w_down

def second_inputs(seed: int = 0) -> dict:
    key = jax.random.key(seed)
    ks = jax.random.split(key, 26)
    f32 = jnp.float32

    def nrm(k, shape, scale):
        return jax.random.normal(k, shape, f32) * scale

    def gain(k, shape):
        return 1.0 + 0.02 * jax.random.normal(k, shape, f32)

    res = (2.0 * DEPTH_2) ** -0.5
    return {
        'x': nrm(ks[0], (BATCH, SEQ, D_MODEL), 1.0),
        'mem': nrm(ks[1], (BATCH, MEM_LEN, D_MODEL), 1.0),
        'norm_mix': gain(ks[2], (DEPTH_2, D_MODEL)),
        'norm_mem': gain(ks[3], (DEPTH_2, D_MODEL)),
        'w_mem_kv': nrm(ks[4], (DEPTH_2, D_MODEL, 2 * MEM_W), D_MODEL ** -0.5),
        'w_out': nrm(ks[5], (DEPTH_2, MIX_W, D_MODEL), MIX_W ** -0.5 * res),
        'norm_ffn': gain(ks[6], (DEPTH_2, D_MODEL)),
        'w_up': nrm(ks[7], (DEPTH_2, D_MODEL, 2 * FFN_DIM), D_MODEL ** -0.5),
        'conv_w': nrm(ks[8], (DEPTH_2, CONV_WIDTH, 2 * FFN_DIM), CONV_WIDTH ** -0.5),
        'conv_b': nrm(ks[9], (DEPTH_2, 2 * FFN_DIM), 0.01),
        'w_down': nrm(ks[10], (DEPTH_2, FFN_DIM, D_MODEL), FFN_DIM ** -0.5 * res),
        'gla_w_in': nrm(ks[11], (N_A_LAYERS, D_MODEL, GLA_IN), D_MODEL ** -0.5),
        'gla_w_gate_up': nrm(ks[12], (N_A_LAYERS, GLA_RANK, GLA_HEADS * GLA_DK), GLA_RANK ** -0.5),
        'gla_b_gate': nrm(ks[13], (N_A_LAYERS, GLA_HEADS * GLA_DK), 0.01),
        'gla_out_norm': gain(ks[14], (N_A_LAYERS, GLA_DV)),
        'nsa_w_in': nrm(ks[15], (N_B_LAYERS, D_MODEL, NSA_IN), D_MODEL ** -0.5),
        'kv_norm': gain(ks[16], (D_MODEL,)),
        'w_kv_shared': nrm(ks[17], (D_MODEL, SHARED_KV_W), D_MODEL ** -0.5),
        'cmp_pos': nrm(ks[18], (2, CMP_BLOCK, NSA_HEAD_DIM), 0.1),
        'cmp_w1': nrm(ks[19], (2, CMP_BLOCK * NSA_HEAD_DIM, CMP_HIDDEN), (CMP_BLOCK * NSA_HEAD_DIM) ** -0.5),
        'cmp_b1': nrm(ks[20], (2, CMP_HIDDEN), 0.01),
        'cmp_w2': nrm(ks[21], (2, CMP_HIDDEN, NSA_HEAD_DIM), CMP_HIDDEN ** -0.5),
        'cmp_b2': nrm(ks[22], (2, NSA_HEAD_DIM), 0.01),
        'rel_bias': nrm(ks[23], (REL_BUCKETS, NSA_HEADS), 0.5),
        'final_norm': gain(ks[24], (D_MODEL,)),
    }

def second_block(x, mem, norm_mix, norm_mem, w_mem_kv, w_out, norm_ffn, w_up, conv_w, conv_b, w_down,
              gla_w_in, gla_w_gate_up, gla_b_gate, gla_out_norm, nsa_w_in, kv_norm, w_kv_shared,
              cmp_pos, cmp_w1, cmp_b1, cmp_w2, cmp_b2, rel_bias, final_norm):
    B, S = x.shape[0], x.shape[1]
    h = x
    shared = None
    for i in range(DEPTH_2):
        if i == N_A_LAYERS:
            shared = shared_kv(h, kv_norm, w_kv_shared, cmp_pos, cmp_w1, cmp_b1, cmp_w2, cmp_b2)
        xn = rmsnorm_2(h, norm_mix[i])
        mem_kv = rmsnorm_2(mem, norm_mem[i]) @ w_mem_kv[i]
        if i < N_A_LAYERS:
            q, k, v, g, lr, mq = split_cols(xn @ gla_w_in[i], GLA_SIZES)
            log_a = jax.nn.log_sigmoid((lr @ gla_w_gate_up[i] + gla_b_gate[i]).astype(jnp.float32)) / GLA_GATE_NORM
            main = gla_mixer(q.reshape(B, S, GLA_HEADS, GLA_DK), k.reshape(B, S, GLA_HEADS, GLA_DK),
                             v.reshape(B, S, GLA_HEADS, GLA_DV), log_a.reshape(B, S, GLA_HEADS, GLA_DK),
                             g.reshape(B, S, GLA_HEADS, GLA_DV), gla_out_norm[i])
        else:
            q, gl, mq = split_cols(xn @ nsa_w_in[i - N_A_LAYERS], NSA_SIZES)
            gates = jax.nn.sigmoid(gl.astype(jnp.float32)).reshape(B, S, NSA_HEADS, 3)
            main = nsa_mixer(q.reshape(B, S, NSA_HEADS, NSA_HEAD_DIM), gates, shared, rel_bias)
        mo = mem_attention(mq, mem_kv)
        h = h + jnp.concatenate([main.astype(xn.dtype), mo.astype(xn.dtype)], axis=-1) @ w_out[i]
        h = h + conv_ffn(rmsnorm_2(h, norm_ffn[i]), w_up[i], conv_w[i], conv_b[i], w_down[i])
    return rmsnorm_2(h, final_norm)


def setup_inputs(seed=0):
    out = dict(first_inputs(seed))
    for name, value in second_inputs(seed + 1).items():
        if name != "x":
            out[name + "_2"] = value
    return out


def reference(
    x, g_mix, w_in, pool_group_w, pool_scale, conv_w, w_branch_pool, w_branch_conv, w_out,
    g_ffn, w_q, sub_keys, expert_u, expert_v, g_final, mem_2, norm_mix_2, norm_mem_2,
    w_mem_kv_2, w_out_2, norm_ffn_2, w_up_2, conv_w_2, conv_b_2, w_down_2, gla_w_in_2,
    gla_w_gate_up_2, gla_b_gate_2, gla_out_norm_2, nsa_w_in_2, kv_norm_2, w_kv_shared_2,
    cmp_pos_2, cmp_w1_2, cmp_b1_2, cmp_w2_2, cmp_b2_2, rel_bias_2, final_norm_2,
):
    x = first_block(
        x, g_mix, w_in, pool_group_w, pool_scale, conv_w, w_branch_pool, w_branch_conv, w_out,
        g_ffn, w_q, sub_keys, expert_u, expert_v, g_final,
    )
    return second_block(
        x, mem_2, norm_mix_2, norm_mem_2, w_mem_kv_2, w_out_2, norm_ffn_2, w_up_2, conv_w_2,
        conv_b_2, w_down_2, gla_w_in_2, gla_w_gate_up_2, gla_b_gate_2, gla_out_norm_2,
        nsa_w_in_2, kv_norm_2, w_kv_shared_2, cmp_pos_2, cmp_w1_2, cmp_b1_2, cmp_w2_2, cmp_b2_2,
        rel_bias_2, final_norm_2,
    )


_drawn_inputs = setup_inputs


def setup_inputs(seed=0):
    import zlib

    import numpy as np

    out = dict(_drawn_inputs(seed))
    spreads = {}
    factors = {'pool_scale': 3.101,
     'norm_mix_2': 5.157,
     'norm_mem_2': 8.0,
     'norm_ffn_2': 4.96,
     'conv_b_2': 8.0,
     'gla_b_gate_2': 8.0,
     'gla_out_norm_2': 8.0,
     'kv_norm_2': 8.0,
     'cmp_pos_2': 20.031,
     'cmp_b1_2': 200.0,
     'cmp_b2_2': 200.0,
     'final_norm_2': 22.917,
     'rel_bias_2': 3.903}
    for name, (base, spread) in spreads.items():
        noise = np.random.default_rng([zlib.crc32(name.encode()), seed]).standard_normal(out[name].shape)
        drawn = base * np.exp(spread * noise) if base else spread * noise
        out[name] = jnp.asarray(drawn.astype(out[name].dtype))
    for name, factor in factors.items():
        out[name] = (out[name] * factor).astype(out[name].dtype)
    return out
```

```python
import concourse.bass as bass
from concourse import mybir
from contextlib import ExitStack

S = 256
D = 1024
KT = D // 128
TT = S // 128
HEADS, TOPK, NKEYS = 8, 16, 128
UNITS = TT * HEADS
NBUF = 8
RING = 4
SLOT = 24 * 128
FT = 2816 // 128
GH, DK, DV, CH = 4, 96, 192, 16
NCH = S // CH
NC = (S - 32) // 16 + 1
EPS = 1e-6
ACT_, DVE_ = "act", "dve"

STREAM = [("win", 16, 2048), ("mix", 4, 2048), ("wout", 4, 2048), ("wq", 8, 2048), ("keys", 1, 2048),
          ("memkv", 4, 2048), ("gla96", 8, 1536), ("glamq", 1, 2048), ("glalr", 1, 128), ("glav", 2, 3072),
          ("wout0", 4, 2560), ("ffn0", FT, 3072), ("kv", 6, 2048), ("nsaq", 4, 2048), ("nsagl", 1, 288),
          ("wout1", 4, 2048), ("ffn1", FT, 3072)]
SLOT0 = {}
_n = 0
for _name, _c, _w in STREAM:
    SLOT0[_name] = _n
    _n += _c

GROUPS = [("mean_x", 1, DVE_), ("mean_mem", 1, DVE_), ("win", 16, ACT_), ("poolmap", 2, ACT_), ("mix", 8, DVE_),
          ("wout", 4, DVE_), ("mean_ffn", 1, DVE_), ("wq", 8, ACT_), ("scores", 8, ACT_), ("memkv", 4, ACT_),
          ("peer_back", 4, DVE_), ("mean_fin", 1, DVE_), ("mean_mix0", 1, DVE_), ("gla_in", 14, ACT_),
          ("gla_gate", 2, ACT_), ("gla_kT", 2, ACT_), ("gla_pair", 8, DVE_), ("gla_sel", 2, ACT_),
          ("gla_intra", 4, ACT_), ("gla_ds", 2 * (NCH - 1), DVE_), ("gla_ms", 2, DVE_), ("wout0", 4, DVE_),
          ("mean_f0", 1, DVE_), ("ffn0", FT, DVE_), ("mean_kv", 1, DVE_), ("kv", 6, ACT_), ("bias", 2, ACT_), ("nsaq", 5, ACT_),
          ("cmp_hid", 2, ACT_), ("cmp_out", 1, DVE_), ("cmp_s", 2 * TT, DVE_), ("cmp_pT", 6, ACT_), ("flip", 6, ACT_),
          ("wout1", 4, DVE_), ("mean_f1", 1, DVE_), ("ffn1", FT, DVE_), ("mean_out", 1, DVE_)]
GROUP0, TAKER, TAKEN = {}, [], []
for _name, _c, _e in GROUPS:
    GROUP0[_name] = len(TAKER)
    for _ in range(_c):
        TAKER.append(_e)
        TAKEN.append(TAKER.count(_e))

USED = []
for _name, _c, _w in STREAM:
    for _s in range(_c):
        if _name in ("win", "wq", "wout", "wout0", "wout1", "memkv", "kv"):
            USED.append(("group", GROUP0[_name] + _s + 1))
        elif _name == "mix":
            USED.append(("group", GROUP0["mix"] + 2 * _s + 2))
        elif _name == "keys":
            USED.append(("group", GROUP0["scores"] + 8))
        elif _name in ("gla96", "glamq", "glalr"):
            USED.append(("group", GROUP0["gla_in"] + _s + 1 + {"gla96": 0, "glamq": 8, "glalr": 9}[_name]))
        elif _name == "glav":
            USED.append(("group", GROUP0["gla_in"] + 12 + 2 * _s))
        elif _name in ("nsaq", "nsagl"):
            USED.append(("group", GROUP0["nsaq"] + _s + (1 if _name == "nsaq" else 5)))
        else:
            USED.append(("down", _s + 1 + (FT if _name == "ffn1" else 0)))

PRM = {}
_n = 0
for _name, _w in [("g_mix", 8), ("g_ffn", 8), ("g_final", 8), ("norm_mix", 16), ("norm_mem", 16), ("norm_ffn", 16),
                  ("kv_norm", 8), ("final_norm", 8), ("pool_scale", 4), ("conv_w", 12), ("ffn_w", 264), ("ffn_b", 88),
                  ("b_gate", 4), ("out_norm", 2), ("cmp_b1", 2), ("cmp_b2k", 1), ("cmp_b2v", 64), ("group_w", 512),
                  ("cmp_w2k", 128), ("cmp_w2v", 64), ("w_gate_up", 384), ("cmp_pos", 64), ("rel", 12)]:
    PRM[_name] = _n
    _n += _w
PRM_W = _n
CST = {}
_n = 0
for _name, _w in [("ident", 128), ("flip", 128), ("mean_d", 128), ("mean_dv", 128), ("place", 240), ("causal", 32),
                  ("iota", 16), ("chunkrow", 8), ("seen", 2)]:
    CST[_name] = _n
    _n += _w
CST_W = _n


class Steps:

    def __init__(self, eng, sem):
        self.eng, self.sem, self.n, self.at = eng, sem, 0, None

    def __call__(self, ins):
        ins.then_inc(self.sem, 1)
        self.n += 1

    def join(self):
        self.eng.wait_ge(self.sem, self.n if self.at is None else self.at + (self.n - self.n0))

    def body(self, i, first, each):
        self.n0, self.each = self.n, each
        self.at = (i - first) * each + self.n

    def left(self, iterations):
        assert self.n - self.n0 == self.each, (self.n - self.n0, self.each)
        self.n = self.n0 + iterations * self.each
        self.at = None


def program(nc, a, out):
    f32, u32, bf16 = mybir.dt.float32, mybir.dt.uint32, mybir.dt.bfloat16
    ALU, ACT, AX = mybir.AluOpType, mybir.ActivationFunctionType, mybir.AxisListType
    X = AX.X
    ctx = ExitStack()
    with ctx:
        def sb(name, shape, dt=f32):
            return ctx.enter_context(nc.sbuf_tensor(name, shape, dt))

        def sem(name):
            return ctx.enter_context(nc.semaphore(name))

        wring = sb("wring", [128, RING, SLOT])
        xT = sb("xT", [128, KT, S])
        hT = sb("hT", [128, KT, S])
        cst = sb("cst", [128, CST_W])
        prm = sb("prm", [128, PRM_W])
        memk = sb("memk", [128, 2, 2, S])
        memv = sb("memv", [128, 2, TT, 256])
        zero = sb("zero", [128, 512], bf16)
        eps = sb("eps", [128, 1])
        AW = 31900
        arena = sb("arena", [128, AW])
        free = {"at": 0}

        def phase(at=0):
            free["at"] = at

        def take(*shape, rows=128):
            n = 1
            for d in shape:
                n *= d
            o = free["at"]
            free["at"] += n
            assert free["at"] <= AW, free["at"]
            v = arena[0:rows, o:o + n]
            if len(shape) == 2:
                v = v.rearrange("p (a b) -> p a b", b=shape[1])
            if len(shape) == 3:
                v = v.rearrange("p (a b c) -> p a b c", b=shape[1], c=shape[2])
            if len(shape) == 4:
                v = v.rearrange("p (a b c d) -> p a b c d", b=shape[1], c=shape[2], d=shape[3])
            return v

        def C(name, w, rows=128):
            return cst[0:rows, CST[name]:CST[name] + w]

        def P(name, i=0, w=1, rows=128):
            return prm[0:rows, PRM[name] + i:PRM[name] + i + w]

        ident = C("ident", 128)

        phase()
        sq = take(KT, S)
        memT = take(KT, S)
        memn = [take(KT, S), take(KT, S)]
        invcnt = take(4, S)
        zp = [take(4, 16 + S) for _ in range(3)]
        pooled = take(4, S)
        poolT = take(4, S)
        zc = take(12, S)
        cu = take(4, 2 + S)
        cy = take(4, S)
        convT = take(4, S)
        zg = take(16, S)
        mixtmp = take(2, 2, S)
        mT = zc[:, 0:KT, :]

        phase(4 * KT * S)
        scores = take(UNITS, 2 * NKEYS)
        G = take(NBUF, 2 * D)
        diag = take(2, 4, 128)
        sc = [take(2, 128), take(2, 128)]
        wk = take(2, 128)
        tv = take(2, 16)
        ti = take(2, 16).bitcast(u32)
        tif = take(2, 16)
        cand = take(16, 16)
        cw = take(16, 16)
        fs = [take(16), take(16)]
        pos = take(16).bitcast(u32)
        pij = take(2, 16).bitcast(u32)
        onehot = take(2, 16 * 16)
        eij = take(2, 16)
        idx = [take(16).bitcast(u32), take(16).bitcast(u32)]
        negm = [take(1), take(1)]
        gexp = [take(16), take(16)]
        gsum = [take(1), take(1)]
        ginv = take(1)
        gate = [take(16), take(16)]
        dot = [take(16), take(16)]
        act4 = [take(4), take(4)]
        wv = [take(16), take(16)]
        qTa = arena[:, 0:16 * S].rearrange("p (a b) -> p a b", b=S)
        peer_o = arena[:, 0:TT * D].rearrange("p (a b) -> p a b", b=D)

        phase()
        sqC = take(KT, S)
        gq = take(GH, S, rows=DK)
        gk = take(GH, S, rows=DK)
        gg = take(2 * GH, S, rows=DK)
        gmq = take(2, S)
        glr = take(S, rows=16)
        gv = take(TT, GH * DV)
        reset = take(GH * S, rows=DK)
        xg = take(GH, S, rows=DK)
        ge = take(GH, S, rows=DK)
        cs = take(GH, S, rows=DK)
        qin = take(GH, S, rows=DK)
        kout = take(GH, S, rows=DK)
        koT = take(TT, GH * DK)
        kom = take(2, GH * DK)
        pw = [take(8, CH, CH, rows=DK) for _ in range(2)]
        pm = take(GH, NCH, 2, CH)
        bd = take(TT, GH, 128)
        intra = take(2 * GH, S, rows=DK)
        state = take(2, GH, DV, rows=DK)
        moT = take(2, S)
        attE = take(2, 2, S)
        attP = take(2, 4, 128)
        attm = take(2, 2)
        atts = take(2, 2)
        attr = take(2, 2)
        gout = sqC[0:DK]

        phase()
        sqF = take(KT, S)
        fy = take(2, 2, S)
        fsa = take(2, S)
        fh = take(2, S)

        phase()
        biasT = take(12, S)
        phase()
        sqE = take(KT, S)
        xn1 = take(KT, S)
        onehots = take(896, rows=33)
        tb = take(896, rows=12)
        hank = take(12, S)
        biasC = take(12, S, rows=NC)
        kvc = take(2, 2, S)
        ksw = take(2, 2, S)
        vsw = take(2, TT, 256)
        nq = take(6, S)
        nmq = take(2, S)
        ngl = take(TT, 36)
        kcT = take(2, NC)
        vc = take(256, rows=NC)
        hid = take(2, 60)
        cE = take(TT, 12 * NC)
        cm = take(TT, 12)
        csum = take(TT, 12)
        cr = take(TT, 12)
        gcmp = take(TT, 12)
        nm = take(2, 2)
        ns = take(2, 2)
        nr = take(2, 2)
        tpos = take(2, 32, 30)
        w1_at = free["at"]
        w1 = take(2, 32, 128)
        phase(w1_at)
        pcT = take(TT, 12, 128, rows=NC)
        naT = take(6, S)
        moT1 = take(2, S)
        nE = take(2, 2, S)
        nP = take(2, 4, 128)

        bank = [ctx.enter_context(nc.psum_tensor(f"bank{b}", [128, 512], f32)) for b in range(4)]
        wide = ctx.enter_context(nc.psum_tensor("wide", [128, 4, 512], f32))

        loaded = sem("loaded")
        late = sem("late")
        w_full = [sem(f"w_full{r}") for r in range(RING)]
        group_full = sem("group_full")
        freed = {ACT_: sem("freed_by_act"), DVE_: sem("freed_by_dve")}
        zeroed = sem("zeroed")
        fence = {e: sem(f"fence_{e}") for e in ("pool", "dve")}
        squared = sem("squared")
        rooted = sem("rooted")
        normed = sem("normed")
        sact, sdve = sem("act_steps"), sem("dve_steps")
        pool_done, conv_done = sem("pool_done"), sem("conv_done")
        mixed = sem("mixed")
        added = sem("added")
        h2_ready = sem("h2_ready")
        sc_ready, idx_ready, fs_ready, gexp_ready = sem("sc_ready"), sem("idx_ready"), sem("fs_ready"), sem("gexp_ready")
        g_full = [sem(f"g_full{b}") for b in range(NBUF)]
        dots, gelu, wts, diags, v_used = sem("dots"), sem("gelu"), sem("wts"), sem("diags"), sem("v_used")
        peer_sum, peer_out = sem("peer_sum"), sem("peer_out")
        bias_dram = sem("bias_dram")
        g_x, g_l, g_cs, g_kout, g_dif, g_exp, g_pw, g_pair = [sem(n) for n in (
            "gate_logits", "gate_logs", "gate_sums", "k_out", "gla_diff", "gla_decay", "gla_weighted", "gla_paired")]
        g_mask, g_sel, g_kom, g_state, g_o, g_sq, g_out = [sem(n) for n in (
            "gla_masked", "gla_placed", "k_chunk", "state_ready", "inter_done", "o_squared", "gla_out")]
        g_eb, g_pre, state_zero = sem("gla_exp_b"), sem("gla_inter"), sem("state_zero")
        a_s, a_m, a_e, a_p, a_t, a_c, a_o, a_done = [sem(n) for n in (
            "att_scores", "att_max", "att_exp", "att_probs", "att_turned", "att_probsT", "att_sum", "att_out")]
        f_lin, f_conv, f_silu, f_hid, f_down, f_sum = [sem(n) for n in (
            "ffn_lin", "ffn_conv", "ffn_silu", "ffn_hidden", "ffn_down", "ffn_summed")]
        c_pos, c_hid, c_kv, c_e, c_x, c_p = [sem(n) for n in (
            "cmp_windows", "cmp_hidden", "cmp_kv", "cmp_shifted", "cmp_exp", "cmp_probs")]
        stored = sem("stored")

        JOBS = [(0, "mem", h, 1) for h in range(4)]
        JOBS += [(1, "nsa", h, tt) for tt in range(TT) for h in range(12)]
        JOBS += [(1, "mem", h, 1) for h in range(4)]
        JOBS0, JOBS1 = range(0, 4), range(4, len(JOBS))

        def job_bufs(layer):
            return (attE, attP, attm, atts, attr, moT, gmq) if layer == 0 else (nE, nP, nm, ns, nr, moT1, nmq)

        block = ctx.enter_context(nc.Block())

        @block.sync
        def _(sp):
            sp.dma_start(xT[:], a["xT"]).then_inc(loaded, 16)
            sp.dma_start(cst[:], a["cst"]).then_inc(loaded, 16)
            sp.dma_start(prm[:], a["prm"]).then_inc(loaded, 16)
            sp.dma_start(memT, a["memT"]).then_inc(loaded, 16)
            sp.dma_start(invcnt, a["invcnt"]).then_inc(loaded, 16)
            for name, slots, width in STREAM:
                n0 = SLOT0[name]

                def load(slot, s, more=0):
                    if n0 + s >= RING:
                        kind, count = USED[n0 + s - RING]
                        sp.wait_ge(group_full if kind == "group" else f_down, more + count)
                    sp.dma_start(wring[:, (n0 + s) % RING, 0:width], a[name][slot]).then_inc(w_full[(n0 + s) % RING], 16)

                rounds = (slots - RING) // RING if slots >= 3 * RING else 0
                for s in range(RING if rounds else 0):
                    load(s, s)
                if rounds:
                    with sp.Fori(0, rounds) as i:
                        for s in range(RING, 2 * RING):
                            load(i * RING + s, s, i * RING)
                for s in range(RING * (rounds + 1) if rounds else 0, slots):
                    load(s, s)
            sp.wait_ge(normed, 11)
            sp.dma_start(out, hT[:]).then_inc(stored, 16)
            sp.wait_ge(stored, 16)

        @block.gpsimd
        def _(pool):
            def gather(par, u, first):
                pool.wait_ge(idx_ready, u + 1)
                pool.sem_inc(fence["pool"])
                for s in range(TOPK):
                    b = s % NBUF
                    if not (first and s < NBUF):
                        pool.wait_ge(v_used, 16 * u + (s - NBUF + 1))
                        pool.sem_inc(fence["pool"])
                    pool.indirect_dma_start(out=G[:, b, :], out_offset=None, in_=a["uv"],
                                            in_offset=bass.IndirectOffsetOnAxis(ap=idx[par][:, s:s + 1], axis=0),
                                            bounds_check=NKEYS * NKEYS - 1, oob_is_err=True).then_inc(g_full[b], 16)

            pool.wait_ge(normed, 4)
            gather(0, 0, True)
            gather(1, 1, False)
            with pool.Fori(1, UNITS // 2) as i:
                gather(0, 2 * i, False)
                gather(1, 2 * i + 1, False)
            pool.wait_ge(added, 12)
            pool.dma_start(reset, a["reset"]).then_inc(late, 16)
            pool.wait_ge(added, 20)
            pool.dma_start(onehots, a["onehot"]).then_inc(late, 16)
            pool.dma_start(w1, a["w1"]).then_inc(late, 16)
            pool.wait_ge(freed[ACT_], TAKEN[GROUP0["bias"] + 1])
            pool.dma_start(a["rows"], tb).then_inc(bias_dram, 16)
            pool.wait_ge(bias_dram, 16)
            rows = a["rows"].tensor
            pool.dma_start(hank, bass.AP(rows, 512, [[1, 128], [896, 12], [1, S]])).then_inc(late, 16)
            pool.dma_start(biasC, bass.AP(rows, 0, [[16, NC], [896, 12], [1, S]])).then_inc(late, 16)

        @block.scalar
        def _(act):
            steps = Steps(act, sact)

            def copy(o, i, scale=1.0, func=ACT.Copy, bias=None):
                kw = {"bias": bias} if bias is not None else {}
                return nc.scalar.activation(o, i, func, scale=scale, **kw)

            def full(stage, i=0):
                act.wait_ge(group_full, GROUP0[stage] + i + 1)
                return bank[(GROUP0[stage] + i) % 4]

            def halves(b, rows=128):
                return b[0:rows, :].rearrange("p (a t) -> p a t", a=2)

            def square(o, i, waits):
                for s_, v_ in waits:
                    act.wait_ge(s_, v_)
                copy(o, i, func=ACT.Square).then_inc(squared, 1)

            def root(stage, i=0, rows=128, n=S):
                b = full(stage, i)[0:rows, 0:n]
                copy(b, b, func=ACT.Sqrt, bias=eps[0:rows]).then_inc(rooted, 1)

            square(sq, xT[:], [(loaded, 80)])
            act.wait_ge(zeroed, 6)
            root("mean_x")
            square(sq, memT, [])
            root("mean_mem")
            for i in range(8):
                b = full("win", i)
                if i == 0:
                    act.wait_ge(zeroed, 4)
                dst = zp[0][:, 2 * i:2 * i + 2, 16:16 + S] if i < 2 else zc[:, 2 * i - 4:2 * i - 2, :]
                copy(dst, halves(b)).then_inc(freed[ACT_], 1)
            with act.Fori(2, 4) as i:
                for s in range(4):
                    act.wait_ge(group_full, i * 4 + (GROUP0["win"] + s + 1))
                    copy(zg[:, bass.ds(i * 8 + (2 * s - 16), 2), :], halves(bank[(GROUP0["win"] + s) % 4]),
                         func=ACT.Sigmoid).then_inc(freed[ACT_], 1)
            for i in range(2):
                b = full("poolmap", i)
                for j in range(2):
                    ins = copy(poolT[:, 2 * i + j, :], b[:, j * S:(j + 1) * S], scale=P("pool_scale", 2 * i + j))
                ins.then_inc(freed[ACT_], 1)
            square(sq, xT[:], [(added, 4), (normed, 3)])
            root("mean_ffn")
            for i in range(8):
                copy(qTa[:, 2 * i:2 * i + 2, :], halves(full("wq", i))).then_inc(freed[ACT_], 1)
            for i in range(8):
                copy(scores[:, 2 * i:2 * i + 2, :], halves(full("scores", i))).then_inc(freed[ACT_], 1)
            act.wait_ge(freed[ACT_], 18 + 16)
            copy(sc[0], scores[:, 0, :].rearrange("p (a b) -> p a b", a=2)).then_inc(sc_ready, 1)
            for l in range(2):
                copy(memk[:, l], halves(full("memkv", 2 * l))).then_inc(freed[ACT_], 1)
                copy(memv[:, l], halves(full("memkv", 2 * l + 1))).then_inc(freed[ACT_], 1)

            def unit(par, u, first, last):
                if not last:
                    act.wait_ge(idx_ready, u + 1)
                    nxt = scores[:, u + 1, :] if isinstance(u, int) else scores[:, bass.ds(u + 1, 1), :].rearrange(
                        "p o n -> p (o n)")
                    copy(sc[1 - par].rearrange("p a b -> p (a b)"), nxt).then_inc(sc_ready, 1)
                act.wait_ge(fs_ready, u + 1)
                nc.scalar.activation(gexp[par], fs[par], ACT.Exp, bias=negm[par],
                                     accum_out=gsum[par]).then_inc(gexp_ready, 1)
                for q in range(4):
                    act.wait_ge(dots, u * 16 + (4 * q + 4))
                    copy(act4[q % 2], dot[par][:, 4 * q:4 * q + 4], func=ACT.Gelu).then_inc(gelu, 1)
                    act.wait_ge(wts, u * 4 + (q + 1))
                    if not (first and q < 2):
                        act.wait_ge(v_used, u * 16 + (4 * q - 4))
                    for e in range(4):
                        ins = copy(diag[:, q % 2, e, :], ident, scale=wv[par][:, 4 * q + e:4 * q + e + 1])
                    ins.then_inc(diags, 1)

            unit(0, 0, True, False)
            unit(1, 1, False, False)
            with act.Fori(1, UNITS // 2 - 1) as i:
                unit(0, 2 * i, False, False)
                unit(1, 2 * i + 1, False, False)
            unit(0, UNITS - 2, False, False)
            unit(1, UNITS - 1, False, True)

            square(sq, xT[:], [(added, 8)])
            root("mean_fin")
            square(sqC, hT[:], [(normed, 5)])
            root("mean_mix0")
            for i in range(14):
                b = full("gla_in", i)
                if i < 2:
                    ins = copy(gq[:, 2 * i:2 * i + 2, :], halves(b, DK), scale=float(DK) ** -0.5)
                elif i < 4:
                    ins = copy(gk[:, 2 * i - 4:2 * i - 2, :], halves(b, DK))
                elif i < 8:
                    ins = copy(gg[:, 2 * i - 8:2 * i - 6, :], halves(b, DK), func=ACT.Silu)
                elif i == 8:
                    ins = copy(gmq, halves(b), scale=0.125)
                elif i == 9:
                    ins = copy(glr, b[0:16, 0:S])
                else:
                    c, t = divmod(i - 10, 2)
                    ins = copy(gv[:, t, 384 * c:384 * c + 384], b[:, 0:384])
                ins.then_inc(freed[ACT_], 1)
            for h in range(GH):
                b = full("gla_gate", h // 2)
                ins = copy(xg[:, h, :], b[0:DK, (h % 2) * S:(h % 2 + 1) * S], func=ACT.Identity, bias=P("b_gate", h, rows=DK))
                if h % 2:
                    ins.then_inc(freed[ACT_], 1)
                else:
                    steps(ins)
            steps.join()
            act.wait_ge(freed[ACT_], TAKEN[GROUP0["gla_gate"] + 1])
            steps(copy(ge, xg, func=ACT.Abs))
            steps.join()
            steps(copy(ge, ge, func=ACT.Exp, scale=-1.0))
            steps.join()
            copy(ge, ge, func=ACT.Ln, bias=1.0).then_inc(g_l, 1)
            act.wait_ge(g_cs, 2)
            copy(ge, cs, func=ACT.Exp, scale=1.0 / 16).then_inc(g_eb, 1)
            copy(kout, xg, func=ACT.Exp, scale=1.0 / 16).then_inc(g_eb, 1)
            for t in range(TT):
                copy(koT[:, t, :], full("gla_kT", t)[:, 0:GH * DK]).then_inc(freed[ACT_], 1)
            for n in range(8):
                act.wait_ge(g_dif, n + 1)
                steps(copy(pw[n % 2], pw[n % 2], func=ACT.Relu, scale=-1.0))
                steps.join()
                copy(pw[n % 2], pw[n % 2], func=ACT.Exp, scale=-1.0 / 16).then_inc(g_exp, 1)
            for t in range(TT):
                copy(bd[:, t], full("gla_sel", t)[:].rearrange("p (h q) -> p h q", h=GH)).then_inc(freed[ACT_], 1)
            for h in range(GH):
                copy(intra[:, 2 * h:2 * h + 2, :], halves(full("gla_intra", h), DK)).then_inc(freed[ACT_], 1)
            for c in range(NCH - 1):
                if c >= 2:
                    act.wait_ge(group_full, GROUP0["gla_ds"] + 2 * (c - 1))
                elif c == 0:
                    act.wait_ge(freed[ACT_], TAKEN[GROUP0["gla_kT"] + 1])
                copy(kom[:, c % 2, :], koT[:, c // 8, :],
                     scale=cst[:, CST["chunkrow"] + c % 8:CST["chunkrow"] + c % 8 + 1]).then_inc(g_kom, 1)
            act.wait_ge(g_o, 1)
            copy(sqC[0:DK], intra, func=ACT.Square).then_inc(g_sq, 1)
            for i in range(2):
                root("gla_ms", i, DK, 2 * S)

            def expo(J):
                layer, kind, h, tt = JOBS[J]
                E, _, m, s_, _, _, _ = job_bufs(layer)
                w = S if kind == "mem" else 128 * (tt + 1)
                act.wait_ge(a_m, J + 1)
                for j in range(2):
                    src = wide[:, J % 2, j * S:j * S + w] if kind == "mem" else E[:, J % 2, j, 0:w]
                    if j == 0 and J - 2 >= (0 if layer == 0 else JOBS1.start):
                        act.wait_ge(a_t, J - 1)
                    ins = nc.scalar.activation(E[:, J % 2, j, 0:w], src, ACT.Exp, bias=m[:, J % 2, j:j + 1],
                                               accum_out=s_[:, J % 2, j:j + 1])
                ins.then_inc(a_e, 1)

            def outs(J):
                layer, kind, h, tt = JOBS[J]
                _, Pt, _, _, _, mo, _ = job_bufs(layer)
                blocks = 4 if kind == "mem" or tt == 1 else 2
                act.wait_ge(a_t, J + 1)
                copy(Pt[:, J % 2, 0:blocks, :], wide[:, 2, 0:blocks * 128].rearrange("p (a b) -> p a b", b=128)).then_inc(a_c, 1)
                act.wait_ge(a_o, J + 1)
                cols = slice(tt * 128, tt * 128 + 128)
                if kind == "mem":
                    lo = 64 * (h % 2)
                    copy(mo[lo:lo + 64, h // 2, :], wide[lo:lo + 64, 3, 0:S]).then_inc(a_done, 1)
                else:
                    g, r = divmod(h, 3)
                    lo = 64 * (g % 2)
                    copy(naT[lo:lo + 64, (g // 2) * 3 + r, cols], wide[lo:lo + 64, 3, 0:128]).then_inc(a_done, 1)

            def attend(jobs):
                expo(jobs[0])
                for J in jobs:
                    if J + 1 in jobs:
                        expo(J + 1)
                    outs(J)

            act.wait_ge(g_out, 1)
            attend(JOBS0)

            def ffn(stage, layer):
                steps.join()
                g0, k0 = GROUP0[stage], layer * FT

                def lin(j, k):
                    act.wait_ge(group_full, j + (g0 + 1))
                    if not isinstance(j, int) or j >= 2 or layer:
                        act.wait_ge(f_hid, j + (k0 - 1))
                    b = bank[(g0 + k) % 4]
                    wcol = PRM["ffn_w"] + layer * 132
                    bcol = PRM["ffn_b"] + layer * 44
                    for c in range(2):
                        if isinstance(j, int):
                            o = c * FT + j
                            w2_, b_ = prm[:, wcol + 3 * o + 2:wcol + 3 * o + 3], prm[:, bcol + o:bcol + o + 1]
                        else:
                            w2_ = prm[:, bass.ds(j * 3 + (wcol + 3 * c * FT + 2), 1)]
                            b_ = prm[:, bass.ds(j + (bcol + c * FT), 1)]
                        ins = copy(fy[:, k % 2, c, :], b[:, c * S:(c + 1) * S], func=ACT.Identity, scale=w2_, bias=b_)
                    ins.then_inc(f_lin, 1)

                def silu(j, k):
                    act.wait_ge(f_conv, j + (k0 + 1))
                    copy(fsa[:, k % 2, :], fy[:, k % 2, 0, :], func=ACT.Silu).then_inc(f_silu, 1)

                for j in range(2):
                    lin(j, j)
                    silu(j, j)
                with act.Fori(0, (FT - 2) // 4) as i:
                    for s in range(4):
                        lin(i * 4 + (s + 2), s + 2)
                        silu(i * 4 + (s + 2), s + 2)

            square(sqF, xT[:], [(added, 16)])
            root("mean_f0")
            ffn("ffn0", 0)
            square(sqE, xT[:], [(added, 20)])
            root("mean_kv")
            for i in range(6):
                b = halves(full("kv", i))
                dst = kvc[:, i] if i < 2 else ksw[:, i - 2] if i < 4 else vsw[:, i - 4]
                copy(dst, b).then_inc(freed[ACT_], 1)
            for i in range(2):
                n = 512 if i == 0 else 384
                copy(tb[:, 512 * i:512 * i + n], full("bias", i)[0:12, 0:n])\
                    .then_inc(freed[ACT_], 1)
            for i in range(5):
                b = full("nsaq", i)
                if i < 3:
                    ins = copy(nq[:, 2 * i:2 * i + 2, :], halves(b), scale=0.125)
                elif i == 3:
                    ins = copy(nmq, halves(b), scale=0.125)
                else:
                    ins = copy(ngl, b[:, 0:72].rearrange("p (t g) -> p t g", t=TT), func=ACT.Sigmoid)
                ins.then_inc(freed[ACT_], 1)
            for base in range(2):
                b = full("cmp_hid", base)
                for kind in range(2):
                    ins = copy(hid[:, kind, 30 * base:30 * base + 30], b[:, 30 * kind:30 * kind + 30], func=ACT.Silu,
                               bias=P("cmp_b1", kind))
                ins.then_inc(freed[ACT_], 1)
            for t in range(TT):
                act.wait_ge(c_e, 2 * t + 2)
                copy(cE[:, t, :], cE[:, t, :], func=ACT.Exp).then_inc(c_x, 1)
            for n in range(6):
                t, c = divmod(n, 3)
                copy(pcT[:, t, 4 * c:4 * c + 4, :], full("cmp_pT", n)[0:NC, :].rearrange("p (h q) -> p h q", h=4))\
                    .then_inc(freed[ACT_], 1)
            for n in range(6):
                copy(biasT[:, 2 * n:2 * n + 2, :], halves(full("flip", n))).then_inc(freed[ACT_], 1)
            attend(JOBS1)
            square(sqF, xT[:], [(added, 24)])
            root("mean_f1")
            ffn("ffn1", 1)
            square(sqF, xT[:], [(added, 28)])
            root("mean_out")

        @block.vector
        def _(dve):
            steps = Steps(dve, sdve)
            V = nc.vector

            def full(stage, i=0):
                dve.wait_ge(group_full, GROUP0[stage] + i + 1)
                return bank[(GROUP0[stage] + i) % 4]

            def halves(b, rows=128):
                return b[0:rows, :].rearrange("p (a t) -> p a t", a=2)

            def norm(stage, src, outs):
                b = full(stage)
                norm.n += 1
                dve.wait_ge(rooted, norm.n)
                steps(V.reciprocal(b[:, 0:S], b[:, 0:S]))
                steps.join()
                for dst, gain, col in outs:
                    for k in range(KT):
                        ins = V.scalar_tensor_tensor(out=dst[:, k, :], in0=src[:, k, :], scalar=P(gain, col + k),
                                                     in1=b[:, 0:S], op0=ALU.mult, op1=ALU.mult)
                    ins.then_inc(normed, 1)
                dve.drain().then_inc(freed[DVE_], 1)

            norm.n = 0
            V.memset(zero[:], 0.0).then_inc(zeroed, 1)
            for z in zp:
                V.memset(z[:, :, 0:16], 0.0).then_inc(zeroed, 1)
            V.memset(cu[:, :, 0:2], 0.0).then_inc(zeroed, 1)
            V.memset(eps[:], EPS).then_inc(zeroed, 1)
            dve.wait_ge(loaded, 80)
            norm("mean_x", xT, [(hT, "g_mix", 0)])
            norm("mean_mem", memT, [(memn[0], "norm_mem", 0), (memn[1], "norm_mem", 8)])
            dve.wait_ge(freed[ACT_], 2)
            dve.wait_ge(zeroed, 5)
            src = zp[0]
            for g in range(4):
                dst = zp[1 + g % 2]
                sh = 1 << g
                steps(V.tensor_tensor(dst[:, g:4, 16:16 + S], src[:, g:4, 16:16 + S], src[:, g:4, 16 - sh:16 - sh + S], ALU.add))
                steps.join()
                steps(V.tensor_tensor(pooled[:, g, :], dst[:, g, 16:16 + S], invcnt[:, g, :], ALU.mult))
                steps.join()
                src = dst
            V.tensor_tensor(pooled, pooled, zp[0][:, :, 16:16 + S], ALU.subtract).then_inc(pool_done, 1)
            dve.wait_ge(freed[ACT_], 8)
            steps(V.tensor_tensor(cu[:, :, 2:2 + S], zc[:, 0:4, :], zc[:, 8:12, :], ALU.mult))
            steps.join()
            for t in range(4):
                steps(V.tensor_scalar(cy[:, t, :], cu[:, t, 2:2 + S], P("conv_w", 3 * t + 2), None, ALU.mult))
            steps.join()
            for tap in (1, 0):
                for t in range(4):
                    steps(V.scalar_tensor_tensor(out=cy[:, t, :], in0=cu[:, t, tap:tap + S], scalar=P("conv_w", 3 * t + tap),
                                                 in1=cy[:, t, :], op0=ALU.mult, op1=ALU.add))
                steps.join()
            V.tensor_tensor(convT, cy, zc[:, 4:8, :], ALU.mult).then_inc(conv_done, 1)
            dve.wait_ge(freed[ACT_], 18)
            dve.wait_ge(conv_done, 1)
            for m in range(KT):
                b = full("mix", m)
                if m >= 2:
                    dve.wait_ge(mixed, m - 1)
                V.tensor_tensor(mixtmp[:, m % 2], halves(b), zg.rearrange("p (g k) t -> p g k t", g=2)[:, :, m, :],
                                ALU.mult).then_inc(freed[DVE_], 1)
                dve.wait_ge(freed[DVE_], TAKEN[GROUP0["mix"] + m])
                V.tensor_tensor(mT[:, m, :], mixtmp[:, m % 2, 0, :], mixtmp[:, m % 2, 1, :], ALU.add).then_inc(mixed, 1)

            def add_groups(stage):
                for i in range(4):
                    b = full(stage, i)
                    V.tensor_tensor(xT[:, 2 * i:2 * i + 2, :], halves(b), xT[:, 2 * i:2 * i + 2, :], ALU.add)\
                        .then_inc(added, 1)
                    add_groups.n += 1
                    dve.drain().then_inc(freed[DVE_], 1)
            add_groups.n = 0

            add_groups("wout")
            norm("mean_ffn", xT, [(hT, "g_ffn", 0)])

            def join():
                steps.join()
                dve.sem_inc(fence["dve"])

            def topk16(vals, ixs, src, work, n):
                for p in range(n):
                    steps(V.max(vals[p][:, 0:8], src[p]))
                join()
                for p in range(n):
                    steps(V.max_index(ixs[p][:, 0:8], vals[p][:, 0:8], src[p]))
                    steps(V.match_replace(work[p], vals[p][:, 0:8], src[p], -3.0e38))
                join()
                for p in range(n):
                    steps(V.max(vals[p][:, 8:16], work[p]))
                join()
                for p in range(n):
                    steps(V.max_index(ixs[p][:, 8:16], vals[p][:, 8:16], work[p]))
                steps.join()

            def select(par, u):
                dve.wait_ge(sc_ready, u + 1)
                dve.sem_inc(fence["dve"])
                topk16([tv[:, p, :] for p in range(2)], [ti[:, p, :] for p in range(2)],
                       [sc[par][:, p, :] for p in range(2)], [wk[:, p, :] for p in range(2)], 2)
                steps(V.tensor_copy(tif, ti))
                steps(V.tensor_tensor(cand, tv[:, 0, :].unsqueeze(2).broadcast_to([128, 16, 16]),
                                      tv[:, 1, :].unsqueeze(1).broadcast_to([128, 16, 16]), ALU.add))
                join()
                flat = cand.rearrange("p a b -> p (a b)")
                topk16([fs[par]], [pos], [flat], [cw.rearrange("p a b -> p (a b)")], 1)
                V.tensor_scalar(negm[par], fs[par][:, 0:1], -1.0, None, ALU.mult).then_inc(fs_ready, 1)
                steps(V.tensor_scalar(pij[:, 0, :], pos, 4, 15, ALU.logical_shift_right, ALU.bitwise_and))
                steps(V.tensor_scalar(pij[:, 1, :], pos, 15, 15, ALU.bitwise_and, ALU.bitwise_and))
                steps.join()
                for p in range(2):
                    oh = onehot[:, p, :].rearrange("p (k i) -> p k i", k=16)
                    steps(V.tensor_tensor(oh, pij[:, p, :].unsqueeze(2).broadcast_to([128, 16, 16]),
                                          C("iota", 16).unsqueeze(1).broadcast_to([128, 16, 16]), ALU.is_equal))
                steps.join()
                for p in range(2):
                    oh = onehot[:, p, :].rearrange("p (k i) -> p k i", k=16)
                    steps(V.tensor_tensor(oh, oh, tif[:, p, :].unsqueeze(1).broadcast_to([128, 16, 16]), ALU.mult))
                steps.join()
                steps(V.tensor_reduce(eij.rearrange("p a b -> p (a b)"), onehot.rearrange("p a (k i) -> p (a k) i", k=16),
                                      X, ALU.add))
                steps.join()
                V.scalar_tensor_tensor(out=idx[par], in0=eij[:, 0, :], scalar=float(NKEYS), in1=eij[:, 1, :],
                                       op0=ALU.mult, op1=ALU.add).then_inc(idx_ready, 1)
            SELECT = 2 + 4 + 2 + 2 + 2 + 1 + 2 + 1 + 1 + 2 + 2 + 2 + 1

            def weigh(par, u, tt):
                dve.wait_ge(gexp_ready, u + 1)
                steps(V.reciprocal(ginv, gsum[par]))
                steps.join()
                steps(V.tensor_scalar(gate[par], gexp[par], ginv, None, ALU.mult))
                steps.join()
                for q in range(4):
                    for s in range(4 * q, 4 * q + 4):
                        b = s % NBUF
                        dve.wait_ge(g_full[b], u * 32 + 16 * (s // NBUF + 1))
                        V.tensor_tensor_reduce(out=G[:, b, 0:D], in0=G[:, b, 0:D],
                                               in1=wide[:, 2 * tt:2 * tt + 2, :].rearrange("p a b -> p (a b)"),
                                               scale=1.0, scalar=0.0, op0=ALU.mult, op1=ALU.add,
                                               accum_out=dot[par][:, s:s + 1]).then_inc(dots, 1)
                    dve.wait_ge(gelu, u * 4 + (q + 1))
                    V.tensor_tensor(wv[par][:, 4 * q:4 * q + 4], act4[q % 2], gate[par][:, 4 * q:4 * q + 4],
                                    ALU.mult).then_inc(wts, 1)
            WEIGH = 2

            def keep_sum(tt):
                dve.wait_ge(peer_sum, tt + 1)
                steps(V.tensor_copy(peer_o[:, tt, 0:512], bank[0][:]))
                steps.join()
                V.tensor_copy(peer_o[:, tt, 512:1024], bank[1][:]).then_inc(peer_out, 1)

            dve.wait_ge(h2_ready, 1)
            select(0, 0)
            with dve.Fori(0, HEADS // 2) as i:
                steps.body(i, 0, 2 * (SELECT + WEIGH))
                for par in range(2):
                    select(1 - par, 2 * i + (par + 1))
                    weigh(par, 2 * i + par, 0)
                steps.left(HEADS // 2)
            keep_sum(0)
            with dve.Fori(HEADS // 2, HEADS - 1) as i:
                steps.body(i, HEADS // 2, 2 * (SELECT + WEIGH))
                for par in range(2):
                    select(1 - par, 2 * i + (par + 1))
                    weigh(par, 2 * i + par, 1)
                steps.left(HEADS // 2 - 1)
            select(1, UNITS - 1)
            weigh(0, UNITS - 2, 1)
            weigh(1, UNITS - 1, 1)
            keep_sum(1)
            for n in range(4):
                t, k = divmod(n, 2)
                b = full("peer_back", n)
                o = xT[:, 4 * k:4 * k + 4, t * 128:t * 128 + 128]
                V.tensor_tensor(o, b[:].rearrange("p (k q) -> p k q", k=4), o, ALU.add).then_inc(added, 1)
                add_groups.n += 1
                dve.drain().then_inc(freed[DVE_], 1)
            norm("mean_fin", xT, [(hT, "g_final", 0)])
            dve.wait_ge(squared, 5)
            for k in range(4):
                V.tensor_copy(xT[:, 2 * k:2 * k + 2, :], hT[:, 2 * k:2 * k + 2, :]).then_inc(added, 1)
            add_groups.n += 4
            dve.wait_ge(added, add_groups.n)
            norm("mean_mix0", xT, [(hT, "norm_mix", 0)])

            dve.wait_ge(g_l, 1)
            dve.wait_ge(late, 16)
            steps(V.scalar_tensor_tensor(out=xg, in0=xg, scalar=0.0, in1=ge, op0=ALU.min, op1=ALU.subtract))
            steps.join()
            V.tensor_tensor_scan(cs.rearrange("p h t -> p (h t)"), reset, xg.rearrange("p h t -> p (h t)"), 0.0,
                                 ALU.mult, ALU.add).then_inc(g_cs, 1)
            dve.wait_ge(g_cs, 1)
            csc = cs.rearrange("p h (c j) -> p (h c) j", j=CH)
            V.tensor_tensor(xg.rearrange("p h (c j) -> p (h c) j", j=CH), csc[:, :, CH - 1:CH].broadcast_to([DK, GH * NCH, CH]),
                            csc, ALU.subtract).then_inc(g_cs, 1)
            dve.wait_ge(g_eb, 2)
            steps(V.tensor_tensor(qin, gq, ge, ALU.mult))
            V.tensor_tensor(kout, kout, gk, ALU.mult).then_inc(g_kout, 1)
            csp = wide[0:DK, 0:2, :].rearrange("p a (b t) -> p (a b) t", b=2)
            gkp = wide[0:DK, 2:4, :].rearrange("p a (b t) -> p (a b) t", b=2)
            steps(V.tensor_copy(csp, cs))
            steps(V.tensor_copy(gkp, gk))
            steps.join()
            full8 = [8, CH, CH]

            def difference(n):
                h, c = n // 2, 8 * (n % 2)
                if n >= 2:
                    dve.wait_ge(group_full, GROUP0["gla_pair"] + n - 1)
                src = cs[:, h, c * CH:(c + 8) * CH].rearrange("p (c j) -> p c j", j=CH)
                srp = csp[:, h, c * CH:(c + 8) * CH].rearrange("p (c j) -> p c j", j=CH)
                V.tensor_tensor(pw[n % 2], srp.unsqueeze(3).broadcast_to([DK] + full8),
                                src.unsqueeze(2).broadcast_to([DK] + full8), ALU.subtract).then_inc(g_dif, 1)

            def weighted(n):
                h, c = n // 2, 8 * (n % 2)
                dve.wait_ge(g_exp, n + 1)
                V.tensor_tensor(pw[n % 2], pw[n % 2],
                                gkp[:, h, c * CH:(c + 8) * CH].rearrange("p (c j) -> p c j", j=CH).unsqueeze(2)
                                .broadcast_to([DK] + full8), ALU.mult).then_inc(g_pw, 1)

            def mask_pairs(n):
                h, c = n // 2, 8 * (n % 2)
                b = full("gla_pair", n)
                V.tensor_tensor(pm[:, h, c:c + 8].rearrange("p c e i -> p c (e i)"),
                                b[:, 0:8 * 2 * CH].rearrange("p (c e) -> p c e", c=8),
                                C("causal", 32).unsqueeze(1).broadcast_to([128, 8, 32]), ALU.mult).then_inc(freed[DVE_], 1)

            difference(0)
            for n in range(8):
                if n + 1 < 8:
                    difference(n + 1)
                weighted(n)
                mask_pairs(n)
            V.memset(state[:, 0], 0.0).then_inc(state_zero, 1)
            dve.wait_ge(state_zero, 1)
            for c in range(NCH - 1):
                for hp in range(2):
                    b = full("gla_ds", 2 * c + hp)
                    if hp == 0 and c >= 1:
                        dve.wait_ge(g_pre, c)
                        dve.wait_ge(freed[DVE_], TAKEN[GROUP0["gla_ds"] + 2 * c - 1])
                    for j in range(2):
                        h = 2 * hp + j
                        ins = V.scalar_tensor_tensor(out=state[:, (c + 1) % 2, h, :], in0=state[:, c % 2, h, :],
                                                     scalar=ge[:, h, c * CH + CH - 1:c * CH + CH], in1=b[0:DK, j * DV:(j + 1) * DV],
                                                     op0=ALU.mult, op1=ALU.add)
                    ins.then_inc(freed[DVE_], 1)
            dve.wait_ge(freed[ACT_], TAKEN[GROUP0["gla_intra"] + 3])
            dve.wait_ge(g_pre, NCH)
            V.tensor_tensor(intra, wide[0:DK].rearrange("p a (b t) -> p (a b) t", b=2), intra, ALU.add).then_inc(g_o, 1)
            dve.wait_ge(g_o, 1)
            for h2 in range(2):
                b = full("gla_ms", h2)
                norm.n += 1
                dve.wait_ge(rooted, norm.n)
                steps(V.reciprocal(b[0:DK, :], b[0:DK, :]))
                steps.join()
                for j in range(2):
                    h = 2 * h2 + j
                    for v in range(2):
                        steps(V.scalar_tensor_tensor(out=gg[:, 2 * h + v, :], in0=gg[:, 2 * h + v, :],
                                                     scalar=P("out_norm", v, rows=DK), in1=b[0:DK, j * S:(j + 1) * S],
                                                     op0=ALU.mult, op1=ALU.mult))
                steps.join()
                dve.drain().then_inc(freed[DVE_], 1)
            V.tensor_tensor(gout, intra, gg, ALU.mult).then_inc(g_out, 1)

            def maxi(J):
                layer, kind, h, tt = JOBS[J]
                E, _, m, _, _, _, _ = job_bufs(layer)
                w = S if kind == "mem" else 128 * (tt + 1)
                dve.wait_ge(a_s, J + 1)
                src = wide[:, J % 2, :].rearrange("p (a s) -> p a s", a=2)[:, :, 0:w]
                if J - 2 >= (0 if layer == 0 else JOBS1.start):
                    dve.wait_ge(a_t, J - 1)
                    dve.wait_ge(a_e, J - 1)
                if kind == "nsa":
                    bias = biasT[:, h, S - w:S].unsqueeze(1).broadcast_to([128, 2, w])
                    steps(V.tensor_tensor(E[:, J % 2, :, 0:w], src, bias, ALU.add))
                    steps.join()
                    src = E[:, J % 2, :, 0:w]
                V.tensor_reduce(m[:, J % 2, :], src, X, ALU.max, negate=True).then_inc(a_m, 1)

            def probs(J):
                layer, kind, h, tt = JOBS[J]
                E, _, _, s_, r_, _, _ = job_bufs(layer)
                w = S if kind == "mem" else 128 * (tt + 1)
                dve.wait_ge(a_e, J + 1)
                steps(V.tensor_scalar(r_[:, J % 2, :], s_[:, J % 2, :], 1e-30, None, ALU.max))
                steps.join()
                steps(V.reciprocal(r_[:, J % 2, :], r_[:, J % 2, :]))
                steps.join()
                if kind == "nsa":
                    steps(V.tensor_tensor(r_[:, J % 2, :], r_[:, J % 2, :], ngl[:, tt, 3 * h + 1:3 * h + 3], ALU.mult))
                    steps.join()
                for j in range(2):
                    ins = V.tensor_scalar(E[:, J % 2, j, 0:w], E[:, J % 2, j, 0:w], r_[:, J % 2, j:j + 1], None, ALU.mult)
                ins.then_inc(a_p, 1)

            def attend(jobs):
                maxi(jobs[0])
                for J in jobs:
                    if J + 1 in jobs:
                        maxi(J + 1)
                    probs(J)

            attend(JOBS0)
            add_groups("wout0")
            norm("mean_f0", xT, [(hT, "norm_ffn", 0)])

            def ffn(stage, layer):
                g0, k0 = GROUP0[stage], layer * FT
                d0 = TAKEN[g0] - 1
                wcol = PRM["ffn_w"] + layer * 132

                def tile(j, k):
                    dve.wait_ge(f_lin, j + (k0 + 1))
                    b = bank[(g0 + k) % 4]
                    for tap in (1, 0):
                        sh = 2 - tap
                        for c in range(2):
                            if isinstance(j, int):
                                o = wcol + 3 * (c * FT + j) + tap
                                w_ = prm[:, o:o + 1]
                            else:
                                w_ = prm[:, bass.ds(j * 3 + (wcol + 3 * c * FT + tap), 1)]
                            ins = V.scalar_tensor_tensor(out=fy[:, k % 2, c, sh:S], in0=b[:, c * S:c * S + S - sh], scalar=w_,
                                                         in1=fy[:, k % 2, c, sh:S], op0=ALU.mult, op1=ALU.add)
                            if tap == 0 and c == 0:
                                ins.then_inc(f_conv, 1)
                            elif tap == 0 and c == 1:
                                ins.then_inc(freed[DVE_], 1)
                            else:
                                steps(ins)
                        if tap:
                            steps.join()
                    dve.wait_ge(f_silu, j + (k0 + 1))
                    dve.wait_ge(freed[DVE_], j + (d0 + 1))
                    if not isinstance(j, int) or j >= 2 or layer:
                        dve.wait_ge(f_down, j + (k0 - 1))
                    V.tensor_tensor(fh[:, k % 2, :], fsa[:, k % 2, :], fy[:, k % 2, 1, :], ALU.mult).then_inc(f_hid, 1)

                for j in range(2):
                    tile(j, j)
                with dve.Fori(0, (FT - 2) // 4) as i:
                    steps.body(i, 0, 8)
                    for s in range(4):
                        tile(i * 4 + (s + 2), s + 2)
                    steps.left((FT - 2) // 4)
                dve.wait_ge(f_sum, layer + 1)
                for n in range(4):
                    V.tensor_tensor(xT[:, 2 * n:2 * n + 2, :], wide[:, n, :].rearrange("p (a t) -> p a t", a=2),
                                    xT[:, 2 * n:2 * n + 2, :], ALU.add).then_inc(added, 1)
                add_groups.n += 4
                dve.wait_ge(added, add_groups.n)

            ffn("ffn0", 0)
            norm("mean_kv", xT, [(hT, "kv_norm", 0), (xn1, "norm_mix", 8)])

            dve.wait_ge(freed[ACT_], TAKEN[GROUP0["kv"] + 1])
            for kind in range(2):
                for gp in range(2):
                    base = kvc[:, kind, gp, :]
                    win = bass.AP(base.tensor, base.offset, [list(base.ap[0]), [1, 32], [16, NC]])
                    ps = P("cmp_pos", 32 * kind, 32).unsqueeze(2).broadcast_to([128, 32, NC])
                    ins = V.tensor_tensor(tpos[:, kind, :, gp * NC:(gp + 1) * NC], win, ps, ALU.add)
                    ins.then_inc(c_pos, 1)
            b = full("cmp_out")
            for base in range(2):
                lo = 64 * base
                steps(V.tensor_scalar(kcT[lo:lo + 64].rearrange("p a n -> p (a n)"), b[lo:lo + 64, 30 * base:30 * base + 30],
                                      prm[lo:lo + 64, PRM["cmp_b2k"]:PRM["cmp_b2k"] + 1], None, ALU.add))
            steps.join()
            V.tensor_tensor(vc.rearrange("p (g d) -> p g d", g=4), b[0:NC, 64:320].rearrange("p (g d) -> p g d", g=4),
                            P("cmp_b2v", 0, 64, rows=NC).unsqueeze(1).broadcast_to([NC, 4, 64]), ALU.add)\
                .then_inc(freed[DVE_], 1)
            dve.wait_ge(freed[ACT_], TAKEN[GROUP0["nsaq"] + 4])
            for n in range(2 * TT):
                t, base = divmod(n, 2)
                b = full("cmp_s", n)
                sv = b[:, 0:6 * NC].rearrange("p (h n) -> p h n", h=6)
                mx = cm[:, t, 6 * base:6 * base + 6]
                steps(V.tensor_reduce(mx, sv, X, ALU.max, negate=True))
                steps.join()
                V.tensor_tensor(cE[:, t, 90 * base:90 * base + 90].rearrange("p (h n) -> p h n", h=6), sv,
                                mx.unsqueeze(2).broadcast_to([128, 6, NC]), ALU.add).then_inc(c_e, 1)
                dve.drain().then_inc(freed[DVE_], 1)
            for t in range(TT):
                for base in range(2):
                    steps(V.tensor_copy(gcmp[:, t, 6 * base:6 * base + 6].rearrange("p (g r) -> p g r", g=2),
                                        ngl[:, t, :].rearrange("p (g b r k) -> p b g r k", g=2, b=2, r=3)[:, base, :, :, 0]))
            steps.join()
            for t in range(TT):
                dve.wait_ge(c_x, t + 1)
                ev = cE[:, t, :].rearrange("p (h n) -> p h n", h=12)
                steps(V.tensor_reduce(csum[:, t, :], ev, X, ALU.add))
                steps.join()
                steps(V.tensor_scalar(csum[:, t, :], csum[:, t, :], 1e-30, None, ALU.max))
                steps.join()
                steps(V.reciprocal(cr[:, t, :], csum[:, t, :]))
                steps.join()
                steps(V.scalar_tensor_tensor(out=cr[:, t, :], in0=cr[:, t, :],
                                             scalar=cst[:, CST["seen"] + t:CST["seen"] + t + 1],
                                             in1=gcmp[:, t, :],
                                             op0=ALU.mult, op1=ALU.mult))
                steps.join()
                V.tensor_tensor(ev, ev, cr[:, t, :].unsqueeze(2).broadcast_to([128, 12, NC]), ALU.mult).then_inc(c_p, 1)
            dve.wait_ge(freed[ACT_], TAKEN[GROUP0["flip"] + 5])
            attend(JOBS1)
            add_groups("wout1")
            norm("mean_f1", xT, [(hT, "norm_ffn", 8)])
            ffn("ffn1", 1)
            norm("mean_out", xT, [(hT, "final_norm", 0)])

        @block.tensor
        def _(pe):
            MM = nc.tensor.matmul

            def begin(stage, i=0):
                g = GROUP0[stage] + i
                if g >= 4:
                    pe.wait_ge(freed[TAKER[g - 4]], TAKEN[g - 4])
                return bank[g % 4]

            def slot(name, i):
                n = SLOT0[name] + i
                pe.wait_ge(w_full[n % RING], 16 * (n // RING + 1))
                return wring[:, n % RING, :]

            def mean(stage, src, nsq):
                b = begin(stage)
                pe.wait_ge(squared, nsq)
                for k in range(KT):
                    ins = MM(b[:, 0:S], C("mean_d", 128), src[:, k, :], start=k == 0, stop=k == KT - 1)
                ins.then_inc(group_full, 1)

            def project(w, src, b, rows=128, tiles=2, kt=KT, width=None):
                width = width or rows
                for m in range(tiles):
                    for k in range(kt):
                        ins = MM(b[0:rows, m * S:(m + 1) * S], w[:, (m * kt + k) * width:(m * kt + k) * width + rows],
                                 src[:, k, :], start=k == 0, stop=k == kt - 1)
                return ins

            def done(ins, stage=None):
                ins.then_inc(group_full, 1)

            pe.wait_ge(loaded, 80)
            mean("mean_x", sq, 1)
            mean("mean_mem", sq, 2)
            pe.wait_ge(normed, 1)
            for s in range(4):
                b = begin("win", s)
                done(project(slot("win", s), hT, b))
            with pe.Fori(1, 4) as i:
                for s in range(4):
                    g = GROUP0["win"] + s
                    if s < 4:
                        pe.wait_ge(freed[ACT_], i * 4 + (s - 3))
                    n = SLOT0["win"] + s
                    pe.wait_ge(w_full[n % RING], (i + 1) * 16)
                    done(project(wring[:, n % RING, :], hT, bank[g % 4]))
            pe.wait_ge(pool_done, 1)
            for i in range(2):
                b = begin("poolmap", i)
                for j in range(2):
                    g = 2 * i + j
                    ins = MM(b[:, j * S:(j + 1) * S], P("group_w", 128 * g, 128), pooled[:, g, :], start=True, stop=True)
                done(ins)
            pe.wait_ge(conv_done, 1)
            pe.wait_ge(freed[ACT_], TAKEN[GROUP0["poolmap"] + 1])
            for i in range(4):
                w = slot("mix", i)
                for j in range(2):
                    m = 2 * i + j
                    b = begin("mix", m)
                    for br, src in enumerate((poolT, convT)):
                        for k in range(4):
                            o = ((j * 2 + br) * 4 + k) * 128
                            ins = MM(b[:, br * S:(br + 1) * S], w[:, o:o + 128], src[:, k, :], start=k == 0, stop=k == 3)
                    done(ins)
            pe.wait_ge(mixed, 8)
            for i in range(4):
                b = begin("wout", i)
                done(project(slot("wout", i), mT, b))
            mean("mean_ffn", sq, 3)
            pe.wait_ge(normed, 4)
            for t in range(TT):
                for k in range(KT):
                    ins = nc.tensor.transpose(wide[:, 2 * t + k // 4, (k % 4) * 128:(k % 4 + 1) * 128],
                                              hT[:, k, t * 128:(t + 1) * 128], ident)
            ins.then_inc(h2_ready, 1)
            pe.wait_ge(freed[DVE_], TAKEN[GROUP0["mean_ffn"]])
            with pe.Fori(0, 2) as i:
                for s in range(4):
                    g, n = GROUP0["wq"] + s, SLOT0["wq"] + s
                    pe.wait_ge(freed[ACT_], i * 4 + (TAKEN[g] - 4))
                    pe.wait_ge(w_full[n % RING], i * 16 + 16 * (n // RING + 1))
                    done(project(wring[:, n % RING, :], hT, bank[g % 4]))
            pe.wait_ge(freed[ACT_], TAKEN[GROUP0["wq"] + 7])
            w = slot("keys", 0)
            for i in range(8):
                t, c = divmod(i, 4)
                b = begin("scores", i)
                for j in range(4):
                    hp = 4 * c + j
                    ins = MM(b[:, j * 128:(j + 1) * 128], qTa[:, hp, t * 128:(t + 1) * 128], w[:, hp * 128:(hp + 1) * 128],
                             start=True, stop=True)
                done(ins)
            for l in range(2):
                b = begin("memkv", 2 * l)
                done(project(slot("memkv", 2 * l), memn[l], b))
                b = begin("memkv", 2 * l + 1)
                w = slot("memkv", 2 * l + 1)
                for t in range(TT):
                    for k in range(KT):
                        ins = MM(b[:, t * 256:(t + 1) * 256], memn[l][:, k, t * 128:(t + 1) * 128],
                                 w[:, k * 256:(k + 1) * 256], start=k == 0, stop=k == KT - 1)
                done(ins)
            pe.wait_ge(freed[ACT_], TAKEN[GROUP0["memkv"] + 3])
            pe.wait_ge(zeroed, 1)
            for t in range(TT):
                if t:
                    pe.wait_ge(peer_out, t)
                for e in range(2):
                    MM(bank[e][:], zero[:, 0:128], zero[:], start=True, stop=False)
                with pe.Fori(t * HEADS // 2, (t + 1) * HEADS // 2) as i:
                    for s in range(2 * TOPK):
                        if s % 4 == 0:
                            pe.wait_ge(diags, i * 8 + (s // 4 + 1))
                        for e in range(2):
                            ins = MM(bank[e][:], diag[:, (s // 4) % 2, s % 4, :],
                                     G[:, s % NBUF, D + 512 * e:D + 512 * (e + 1)], start=False, stop=False)
                        ins.then_inc(v_used, 1)
                for e in range(2):
                    ins = MM(bank[e][:], zero[:, 0:128], zero[:], start=False, stop=True)
                ins.then_inc(peer_sum, 1)
            pe.wait_ge(peer_out, 2)
            for n in range(4):
                t, k4 = divmod(n, 2)
                b = begin("peer_back", n)
                for k in range(4):
                    ins = nc.tensor.transpose(b[:, k * 128:(k + 1) * 128],
                                              peer_o[:, t, (4 * k4 + k) * 128:(4 * k4 + k + 1) * 128], ident)
                done(ins)
            mean("mean_fin", sq, 4)
            mean("mean_mix0", sqC, 5)
            pe.wait_ge(normed, 6)
            for i in range(8):
                b = begin("gla_in", i)
                done(project(slot("gla96", i), hT, b, rows=DK))
            b = begin("gla_in", 8)
            done(project(slot("glamq", 0), hT, b))
            b = begin("gla_in", 9)
            done(project(slot("glalr", 0), hT, b, rows=16, tiles=1))
            for c in range(2):
                w = slot("glav", c)
                for t in range(TT):
                    b = begin("gla_in", 10 + 2 * c + t)
                    for k in range(KT):
                        ins = MM(b[:, 0:384], hT[:, k, t * 128:(t + 1) * 128], w[:, k * 384:(k + 1) * 384],
                                 start=k == 0, stop=k == KT - 1)
                    done(ins)
            for h in range(GH):
                if h % 2 == 0:
                    b = begin("gla_gate", h // 2)
                    pe.wait_ge(freed[ACT_], TAKEN[GROUP0["gla_in"] + 9])
                ins = MM(b[0:DK, (h % 2) * S:(h % 2 + 1) * S], P("w_gate_up", DK * h, DK, rows=16), glr, start=True, stop=True)
                if h % 2:
                    done(ins)
            pe.wait_ge(g_kout, 1)
            for t in range(TT):
                b = begin("gla_kT", t)
                for h in range(GH):
                    ins = nc.tensor.transpose(b[:, h * DK:(h + 1) * DK], kout[:, h, t * 128:(t + 1) * 128], ident[0:DK, 0:DK])
                done(ins)
            for n in range(8):
                h, c0 = n // 2, 8 * (n % 2)
                b = begin("gla_pair", n)
                pe.wait_ge(g_pw, n + 1)
                for c in range(8):
                    for e in range(2):
                        ins = MM(b[:, (c * 2 + e) * CH:(c * 2 + e + 1) * CH],
                                 pw[n % 2][:, c, 8 * e:8 * e + 8, :].rearrange("p i j -> p (i j)"),
                                 gq[:, h, (c0 + c) * CH:(c0 + c + 1) * CH], start=True, stop=True)
                done(ins)
            pe.wait_ge(freed[DVE_], TAKEN[GROUP0["gla_pair"] + 7])
            for t in range(TT):
                b = begin("gla_sel", t)
                for h in range(GH):
                    for c in range(8):
                        o = CST["place"] + 112 - 16 * c
                        for e in range(2):
                            ins = MM(b[:, h * 128 + c * CH:h * 128 + (c + 1) * CH], cst[:, o:o + 128],
                                     pm[:, h, 8 * t + c, e, :], start=e == 0, stop=e == 1)
                done(ins)
            pe.wait_ge(freed[ACT_], TAKEN[GROUP0["gla_sel"] + 1])
            for h in range(GH):
                b = begin("gla_intra", h)
                for v in range(2):
                    for t in range(TT):
                        o = h * DV + v * DK
                        ins = MM(b[0:DK, v * S + t * 128:v * S + (t + 1) * 128], gv[:, t, o:o + DK], bd[:, t, h, :],
                                 start=True, stop=True)
                done(ins)
            for c in range(NCH):
                if c < NCH - 1:
                    pe.wait_ge(g_kom, c + 1)
                for hp in range(2 if c < NCH - 1 else 0):
                    b = begin("gla_ds", 2 * c + hp)
                    for j in range(2):
                        h = 2 * hp + j
                        ins = MM(b[0:DK, j * DV:(j + 1) * DV], kom[:, c % 2, h * DK:(h + 1) * DK],
                                 gv[:, c // 8, h * DV:(h + 1) * DV], start=True, stop=True)
                    done(ins)
                if c:
                    pe.wait_ge(freed[DVE_], TAKEN[GROUP0["gla_ds"] + 2 * c - 1])
                else:
                    pe.wait_ge(g_pw, 8)
                    pe.wait_ge(state_zero, 1)
                for h in range(GH):
                    for v in range(2):
                        o = (2 * h + v) * S + c * CH
                        ins = MM(wide[0:DK, o // 512, o % 512:o % 512 + CH], state[:, c % 2, h, v * DK:(v + 1) * DK],
                                 qin[:, h, c * CH:(c + 1) * CH], start=True, stop=True)
                ins.then_inc(g_pre, 1)
            pe.wait_ge(g_sq, 1)
            for h in range(GH):
                if h % 2 == 0:
                    b = begin("gla_ms", h // 2)
                for v in range(2):
                    ins = MM(b[0:DK, (h % 2) * S:(h % 2 + 1) * S], C("mean_dv", DK, rows=DK), sqC[0:DK, 2 * h + v, :],
                             start=v == 0, stop=v == 1)
                if h % 2:
                    done(ins)

            def score(J):
                layer, kind, h, tt = JOBS[J]
                _, _, _, _, _, _, mq = job_bufs(layer)
                if J - 2 >= (0 if layer == 0 else JOBS1.start):
                    pe.wait_ge(a_m, J - 1)
                    pe.wait_ge(a_e, J - 1)
                cols = slice(tt * 128, tt * 128 + 128)
                for j in range(2):
                    if kind == "mem":
                        lo = 64 * (h % 2)
                        ins = MM(wide[:, J % 2, j * S:(j + 1) * S], mq[lo:lo + 64, h // 2, j * 128:(j + 1) * 128],
                                 memk[lo:lo + 64, layer, h // 2, :],
                                 start=True, stop=True)
                    else:
                        g, r = divmod(h, 3)
                        lo, w = 64 * (g % 2), 128 * (tt + 1)
                        ins = MM(wide[:, J % 2, j * S:j * S + w], nq[lo:lo + 64, (g // 2) * 3 + r, cols],
                                 ksw[lo:lo + 64, j, g // 2, 0:w], start=True, stop=True)
                ins.then_inc(a_s, 1)

            def turn(J):
                layer, kind, h, tt = JOBS[J]
                E = job_bufs(layer)[0]
                w = S if kind == "mem" else 128 * (tt + 1)
                pe.wait_ge(a_p, J + 1)
                if J:
                    pe.wait_ge(a_c, J)
                n = 0
                for j in range(2):
                    for k in range(w // 128):
                        ins = nc.tensor.transpose(wide[:, 2, n * 128:(n + 1) * 128], E[:, J % 2, j, k * 128:(k + 1) * 128], ident)
                        n += 1
                ins.then_inc(a_t, 1)

            def values(J):
                layer, kind, h, tt = JOBS[J]
                Pt = job_bufs(layer)[1]
                pe.wait_ge(a_c, J + 1)
                if J:
                    pe.wait_ge(a_done, J)
                if kind == "mem":
                    for j in range(2):
                        for k in range(TT):
                            ins = MM(wide[:, 3, j * 128:(j + 1) * 128], memv[:, layer, k, h // 2 * 128:(h // 2 + 1) * 128],
                                     Pt[:, J % 2, 2 * j + k, :], start=k == 0, stop=k == TT - 1)
                else:
                    g, r = divmod(h, 3)
                    gp = g // 2
                    MM(wide[:, 3, 0:128], vc[:, gp * 128:(gp + 1) * 128], pcT[:, tt, 6 * (g % 2) + 3 * gp + r, :], start=True, stop=False)
                    n = 0
                    for j in range(2):
                        for k in range(tt + 1):
                            ins = MM(wide[:, 3, 0:128], vsw[:, j, k, gp * 128:(gp + 1) * 128], Pt[:, J % 2, n, :],
                                     start=False, stop=n == 2 * tt + 1)
                            n += 1
                ins.then_inc(a_o, 1)

            def attend(jobs):
                score(jobs[0])
                for J in jobs:
                    if J + 1 in jobs:
                        score(J + 1)
                    turn(J)
                    values(J)

            pe.wait_ge(g_out, 1)
            attend(JOBS0)
            pe.wait_ge(a_done, JOBS0.stop)
            for i in range(4):
                b = begin("wout0", i)
                w = slot("wout0", i)
                for m in range(2):
                    for k in range(10):
                        rows = DK if k < 8 else 128
                        src = gout[:, k, :] if k < 8 else moT[:, k - 8, :]
                        o = (m * 10 + k) * 128
                        ins = MM(b[:, m * S:(m + 1) * S], w[0:rows, o:o + 128], src, start=k == 0, stop=k == 9)
                done(ins)

            def ffn(stage, layer):
                g0, n0, k0 = GROUP0[stage], SLOT0[stage], layer * FT
                for n in range(4):
                    MM(wide[:, n, :], zero[:, 0:128], zero[:], start=True, stop=False)
                d0 = TAKEN[g0] - 1

                def up(j, k):
                    pe.wait_ge(freed[DVE_], j + (d0 - 3))
                    n = n0 + k
                    if isinstance(j, int):
                        pe.wait_ge(w_full[n % RING], 16 * ((n0 + j) // RING + 1))
                    else:
                        pe.wait_ge(w_full[n % RING], up.i * 16 + 16 * (n // RING + 1))
                    done(project(wring[:, n % RING, :], hT, bank[(g0 + k) % 4]))

                def down(j, k):
                    pe.wait_ge(f_hid, j + (k0 + 1))
                    w = wring[:, (n0 + k) % RING, :]
                    for m in range(KT):
                        ins = MM(wide[:, m // 2, (m % 2) * S:(m % 2 + 1) * S], w[:, (16 + m) * 128:(17 + m) * 128],
                                 fh[:, k % 2, :], start=False, stop=False)
                    ins.then_inc(f_down, 1)

                up(0, 0)
                with pe.Fori(0, (FT - 2) // 4) as i:
                    up.i = i
                    for s in range(4):
                        up(i * 4 + (s + 1), s + 1)
                        down(i * 4 + s, s)
                up(FT - 1, FT - 1)
                down(FT - 2, FT - 2)
                down(FT - 1, FT - 1)
                for n in range(4):
                    ins = MM(wide[:, n, :], zero[:, 0:128], zero[:], start=False, stop=True)
                ins.then_inc(f_sum, 1)

            mean("mean_f0", sqF, 6)
            pe.wait_ge(normed, 7)
            ffn("ffn0", 0)
            mean("mean_kv", sqE, 7)
            pe.wait_ge(normed, 9)
            for i in range(4):
                b = begin("kv", i)
                done(project(slot("kv", i), hT, b))
            for i in range(4, 6):
                b = begin("kv", i)
                w = slot("kv", i)
                for t in range(TT):
                    for k in range(KT):
                        ins = MM(b[:, t * 256:(t + 1) * 256], hT[:, k, t * 128:(t + 1) * 128], w[:, k * 256:(k + 1) * 256],
                                 start=k == 0, stop=k == KT - 1)
                done(ins)
            pe.wait_ge(late, 48)
            for i in range(2):
                n = 512 if i == 0 else 384
                done(MM(begin("bias", i)[0:12, 0:n], P("rel", 0, 12, rows=33), onehots[:, 512 * i:512 * i + n], start=True, stop=True))
            for i in range(4):
                b = begin("nsaq", i)
                done(project(slot("nsaq", i), xn1, b))
            b = begin("nsaq", 4)
            w = slot("nsagl", 0)
            for t in range(TT):
                for k in range(KT):
                    ins = MM(b[:, t * 36:(t + 1) * 36], xn1[:, k, t * 128:(t + 1) * 128], w[:, k * 36:(k + 1) * 36],
                             start=k == 0, stop=k == KT - 1)
            done(ins)
            pe.wait_ge(c_pos, 4)
            for base in range(2):
                b = begin("cmp_hid", base)
                lo = 64 * base
                for kind in range(2):
                    for l in range(32):
                        ins = MM(b[:, 30 * kind:30 * kind + 30], w1[lo:lo + 64, kind, l, :], tpos[lo:lo + 64, kind, l, :],
                                 start=l == 0, stop=l == 31)
                done(ins)
            b = begin("cmp_out")
            pe.wait_ge(freed[ACT_], TAKEN[GROUP0["cmp_hid"] + 1])
            MM(b[:, 0:60], P("cmp_w2k", 0, 128), hid[:, 0, :], start=True, stop=True)
            for gp in range(2):
                for base in range(2):
                    o = 64 + (2 * gp + base) * 64
                    ins = MM(b[0:NC, o:o + 64], hid[:, 1, base * 30 + gp * NC:base * 30 + (gp + 1) * NC], P("cmp_w2v", 0, 64),
                             start=True, stop=True)
            done(ins)
            pe.wait_ge(freed[DVE_], TAKEN[GROUP0["cmp_out"]])
            pe.wait_ge(late, 80)
            for n in range(2 * TT):
                t, base = divmod(n, 2)
                lo = 64 * base
                b = begin("cmp_s", n)
                for e in range(6):
                    gp, r = divmod(e, 3)
                    MM(b[:, e * NC:(e + 1) * NC], nq[lo:lo + 64, gp * 3 + r, t * 128:(t + 1) * 128],
                       kcT[lo:lo + 64, gp, :], start=True, stop=False)
                    ins = MM(b[:, e * NC:(e + 1) * NC], biasC[:, (2 * gp + base) * 3 + r, t * 128:(t + 1) * 128],
                             cst[0:NC, CST["flip"] + 128 - NC:CST["flip"] + 128], start=False, stop=True)
                done(ins)
            for n in range(6):
                t, c = divmod(n, 3)
                b = begin("cmp_pT", n)
                pe.wait_ge(c_p, t + 1)
                for j in range(4):
                    h = 4 * c + j
                    ins = nc.tensor.transpose(b[0:NC, j * 128:(j + 1) * 128], cE[:, t, h * NC:(h + 1) * NC], ident)
                done(ins)
            for n in range(6):
                b = begin("flip", n)
                done(MM(b[:], C("flip", 128), hank[:, 2 * n:2 * n + 2, :].rearrange("p h t -> p (h t)"), start=True, stop=True))
            pe.wait_ge(freed[ACT_], TAKEN[GROUP0["cmp_pT"] + 5])
            attend(JOBS1)
            pe.wait_ge(a_done, JOBS1.stop)
            for i in range(4):
                b = begin("wout1", i)
                w = slot("wout1", i)
                for m in range(2):
                    for k in range(KT):
                        src = naT[:, k, :] if k < 6 else moT1[:, k - 6, :]
                        o = (m * KT + k) * 128
                        ins = MM(b[:, m * S:(m + 1) * S], w[:, o:o + 128], src, start=k == 0, stop=k == KT - 1)
                done(ins)
            mean("mean_f1", sqF, 8)
            pe.wait_ge(normed, 10)
            ffn("ffn1", 1)
            mean("mean_out", sqF, 9)


def pack(w, width=128):
    kt, nt = w.shape[0] // 128, w.shape[1] // width
    t = w.reshape(kt, 128, nt, width).transpose(2, 1, 0, 3).reshape(nt // 2, 2, 128, kt * width)
    return t.transpose(0, 2, 1, 3).reshape(nt // 2, 128, 2 * kt * width)


def moving(w):
    return w.reshape(w.shape[0] // 128, 128, -1).transpose(1, 0, 2).reshape(1, 128, -1)


def layout(i):
    import numpy as np

    f = np.float32
    cat = np.concatenate
    col = lambda v: v.reshape(-1, 128).T
    L = {}
    L["xT"] = i["x"][0].T.reshape(KT, 128, S).transpose(1, 0, 2)
    L["memT"] = i["mem_2"][0].T.reshape(KT, 128, S).transpose(1, 0, 2)
    L["win"] = pack(i["w_in"][0])
    br = np.stack([w.reshape(4, 128, KT, 128).transpose(2, 1, 0, 3) for w in (i["w_branch_pool"][0], i["w_branch_conv"][0])], 2)
    L["mix"] = br.reshape(4, 2, 128, 1024).transpose(0, 2, 1, 3).reshape(4, 128, 2048)
    L["wout"] = pack(i["w_out"][0])
    L["wq"] = pack(i["w_q"][0])
    L["keys"] = i["sub_keys"][0].transpose(3, 0, 1, 2).reshape(1, 128, 2048)
    mk = i["w_mem_kv_2"]
    L["memkv"] = cat([x for l in range(2) for x in (pack(mk[l][:, 0:256]), moving(mk[l][:, 256:512]))])
    gw = i["gla_w_in_2"][0]
    L["gla96"] = pack(cat([gw[:, 0:768], gw[:, 1536:2304]], 1), DK)
    L["glamq"] = pack(gw[:, 2320:2576])
    L["glalr"] = moving(gw[:, 2304:2320])
    L["glav"] = cat([moving(gw[:, 768:1152]), moving(gw[:, 1152:1536])])
    wo = i["w_out_2"]
    rows = np.zeros((10, 128, D), f)
    rows[0:8, 0:DK] = wo[0][0:768].reshape(8, DK, D)
    rows[8:10] = wo[0][768:].reshape(2, 128, D)
    L["wout0"] = pack(rows.reshape(1280, D))
    for l in range(2):
        up, down = i["w_up_2"][l], i["w_down_2"][l]
        ab = up.reshape(KT, 128, 2, FT, 128).transpose(3, 1, 2, 0, 4).reshape(FT, 128, 2048)
        L[f"ffn{l}"] = cat([ab, down.reshape(FT, 128, D)], 2)
    kv = i["w_kv_shared_2"].reshape(D, 6, 256)
    L["kv"] = cat([pack(kv[:, n]) for n in (0, 1, 2, 4)] + [moving(kv[:, n]) for n in (3, 5)])
    nw = i["nsa_w_in_2"][0]
    perm = lambda w: w.reshape(2, 2, 3, 64, -1).transpose(0, 2, 1, 3, 4).reshape(768, -1)
    L["nsaq"] = cat([pack(np.ascontiguousarray(perm(nw[:, 0:768].T).T)), pack(nw[:, 804:1060])])
    L["nsagl"] = moving(nw[:, 768:804])
    L["wout1"] = pack(cat([perm(wo[1][0:768]), wo[1][768:]]))
    L["uv"] = cat([i["expert_u"][0], i["expert_v"][0]], 1)
    L["w1"] = np.tile(i["cmp_w1_2"].reshape(2, 32, 64, 128).transpose(2, 0, 1, 3), (2, 1, 1, 1))
    p = np.zeros((128, PRM_W), f)

    def put(name, v):
        p[0:v.shape[0], PRM[name]:PRM[name] + v.shape[1]] = v

    put("g_mix", col(i["g_mix"][0]))
    put("g_ffn", col(i["g_ffn"][0]))
    put("g_final", col(i["g_final"]))
    put("norm_mix", col(i["norm_mix_2"]))
    put("norm_mem", col(i["norm_mem_2"]))
    put("norm_ffn", col(i["norm_ffn_2"]))
    put("kv_norm", col(i["kv_norm_2"]))
    put("final_norm", col(i["final_norm_2"]))
    put("pool_scale", col(i["pool_scale"][0]))
    put("conv_w", i["conv_w"][0].reshape(3, 4, 128).transpose(2, 1, 0).reshape(128, 12))
    put("ffn_w", i["conv_w_2"].reshape(2, 3, 2 * FT, 128).transpose(3, 0, 2, 1).reshape(128, -1))
    put("ffn_b", i["conv_b_2"].reshape(2 * 2 * FT, 128).T)
    put("b_gate", i["gla_b_gate_2"][0].reshape(GH, DK).T)
    put("out_norm", i["gla_out_norm_2"][0].reshape(2, DK).T)
    put("cmp_b1", i["cmp_b1_2"].T)
    put("cmp_b2k", np.tile(i["cmp_b2_2"][0], 2)[:, None])
    put("cmp_b2v", np.tile(i["cmp_b2_2"][1][None], (NC, 1)))
    put("group_w", i["pool_group_w"][0].transpose(1, 0, 2).reshape(128, 512))
    put("cmp_w2k", np.tile(i["cmp_w2_2"][0], (1, 2)))
    put("cmp_w2v", i["cmp_w2_2"][1])
    put("w_gate_up", i["gla_w_gate_up_2"][0])
    put("cmp_pos", np.tile(i["cmp_pos_2"].transpose(2, 0, 1).reshape(64, 64), (2, 1)))
    put("rel", cat([i["rel_bias_2"], np.ones((1, 12), f)]))
    L["prm"] = p
    c = np.zeros((128, CST_W), f)
    r = np.arange(128)
    c[r, CST["ident"] + r] = 1
    c[r, CST["flip"] + 127 - r] = 1
    c[:, CST["mean_d"]:CST["mean_d"] + 128] = 1.0 / D
    c[:, CST["mean_dv"]:CST["mean_dv"] + 128] = 1.0 / DV
    c[r, CST["place"] + 112 + r % 16] = 1
    for e in range(2):
        ok = r % 16 <= 8 * e + r // 16
        c[r[ok], (CST["causal"] + 16 * e + 8 * e + r // 16)[ok]] = 1
    c[:, CST["iota"]:CST["iota"] + 16] = np.arange(16)
    c[r, CST["chunkrow"] + r // 16] = 1
    c[31:, CST["seen"]] = 1
    c[:, CST["seen"] + 1] = 1
    L["cst"] = c
    t = np.arange(S)
    L["invcnt"] = np.tile(np.stack([1.0 / np.minimum(t + 1, w) for w in (2, 4, 8, 16)]).astype(f)[None], (128, 1, 1))
    L["reset"] = np.tile((np.arange(GH * S) % CH != 0).astype(f)[None], (DK, 1))
    dist = cat([np.arange(512) - 255, 255 - np.arange(384)])
    far = 16 + (np.log(np.maximum(dist, 1) / 16.0) / np.log(8.0) * 16 + 1e-9).astype(np.int64)
    bucket = np.where(dist < 16, dist, np.minimum(far, 31))
    oh = np.zeros((33, 896), f)
    n = np.arange(896)
    oh[bucket[dist >= 0], n[dist >= 0]] = 1
    oh[32, dist < 0] = -1e30
    L["onehot"] = oh
    return {k: np.ascontiguousarray(v) for k, v in L.items()}


def kernel(**inputs):
    import numpy as np
    import concourse.bacc as bacc
    from concourse.bass_utils import run_bass_kernel_spmd

    nc = bacc.Bacc("TRN2", target_bir_lowering=False, num_devices=1)
    arrays = layout({k: np.asarray(v) for k, v in inputs.items()})
    f32 = mybir.dt.float32
    a = {k: nc.dram_tensor(k + "_dram", v.shape, f32, kind="ExternalInput").ap() for k, v in arrays.items()}
    a["rows"] = nc.dram_tensor("rows_dram", (12, 896), f32, kind="Internal").ap()
    out = nc.dram_tensor("out_dram", (128, KT, S), f32, kind="ExternalOutput").ap()
    program(nc, a, out)
    r = run_bass_kernel_spmd(nc, [{k + "_dram": v for k, v in arrays.items()}], core_ids=[0])
    y = r.results[0]["out_dram"]
    return np.ascontiguousarray(y.transpose(2, 1, 0)).reshape(1, S, D)
```

```python
import concourse.bass as bass
from concourse import mybir
from contextlib import ExitStack

S = 256
D = 1024
KT = D // 128
TT = S // 128
HEADS, TOPK, NKEYS = 8, 16, 128
UNITS = TT * HEADS
NBUF = 8
RING = 4
SLOT = 24 * 128
FT = 2816 // 128
GH, DK, DV = 4, 96, 192
LEVELS = 9
NC = (S - 32) // 16 + 1
LH = 16
EPS = 1e-6
ACT_, DVE_ = "act", "dve"

STREAM = [("win", 16, 2048), ("mix", 4, 2048), ("wout", 4, 2048), ("wqa", 2, 2048), ("keysa", 1, 512), ("wq", 6, 2048), ("keys", 1, 2048),
          ("memkv", 4, 2048), ("gla96", 8, 1536), ("glamq", 1, 2048), ("glalr", 1, 128), ("glav", 2, 3072),
          ("wout0", 4, 2560), ("ffn0", FT, 3072), ("kv", 6, 2048), ("nsaq", 3, 2048), ("nsamq", 1, 2048), ("nsagl", 1, 288),
          ("wout1", 4, 2048), ("ffn1", FT, 3072)]
SLOT0 = {}
_n = 0
for _name, _c, _w in STREAM:
    SLOT0[_name] = _n
    _n += _c

GROUPS = [("bias", 2, ACT_), ("mean_x", 1, DVE_), ("win", 16, ACT_), ("poolmap", 2, ACT_), ("mix", 8, DVE_),
          ("wout", 4, DVE_), ("mean_ffn", 1, DVE_), ("mean_mem", 1, DVE_), ("wqa", 2, ACT_), ("scores_a", 1, ACT_),
          ("wq", 6, ACT_), ("scores", 7, ACT_), ("memkv", 4, ACT_),
          ("peer_back", 4, DVE_), ("mean_fin", 1, DVE_), ("mean_mix0", 1, DVE_), ("gla_in", 14, ACT_),
          ("gla_gate", 2, ACT_), ("gla_pair", 2 * LEVELS - 1, DVE_), ("gla_ms", 2, DVE_), ("wout0", 4, DVE_),
          ("mean_f0", 1, DVE_), ("ffn0", FT, DVE_), ("mean_kv", 1, DVE_), ("flip", 6, ACT_), ("kv", 6, ACT_), ("nsaq", 3, ACT_),
          ("cmp_hid", 1, ACT_), ("nsamq", 1, ACT_), ("cmp_out", 1, DVE_), ("nsagl", 1, ACT_), ("cmp_s", 2 * TT, DVE_),
          ("cmp_pT", 6, ACT_),
          ("wout1", 4, DVE_), ("mean_f1", 1, DVE_), ("ffn1", FT, DVE_), ("mean_out", 1, DVE_)]
GROUP0, TAKER, TAKEN = {}, [], []
for _name, _c, _e in GROUPS:
    GROUP0[_name] = len(TAKER)
    for _ in range(_c):
        TAKER.append(_e)
        TAKEN.append(TAKER.count(_e))

USED = []
for _name, _c, _w in STREAM:
    for _s in range(_c):
        if _name in ("win", "wqa", "wq", "wout", "wout0", "wout1", "memkv", "kv", "nsaq", "nsamq", "nsagl"):
            USED.append(("group", GROUP0[_name] + _s + 1))
        elif _name == "mix":
            USED.append(("group", GROUP0["mix"] + 2 * _s + 2))
        elif _name == "keys":
            USED.append(("group", GROUP0["scores"] + 7))
        elif _name == "keysa":
            USED.append(("group", GROUP0["scores_a"] + 1))
        elif _name in ("gla96", "glamq", "glalr"):
            USED.append(("group", GROUP0["gla_in"] + _s + 1 + {"gla96": 0, "glamq": 8, "glalr": 9}[_name]))
        elif _name == "glav":
            USED.append(("group", GROUP0["gla_in"] + 12 + 2 * _s))
        else:
            USED.append(("down", _s + 1 + (FT if _name == "ffn1" else 0)))

PRM = {}
_n = 0
for _name, _w in [("g_mix", 8), ("g_ffn", 8), ("g_final", 8), ("norm_mix", 16), ("norm_mem", 16), ("norm_ffn", 16),
                  ("kv_norm", 8), ("final_norm", 8), ("pool_scale", 4), ("conv_w", 12), ("ffn_w", 264), ("ffn_b", 88),
                  ("b_gate", 4), ("out_norm", 2), ("cmp_b1", 2), ("cmp_b2k", 1), ("cmp_b2v", 64), ("group_w", 512),
                  ("cmp_w2k", 128), ("cmp_w2v", 64), ("w_gate_up", 384), ("cmp_pos", 64), ("rel", 12)]:
    PRM[_name] = _n
    _n += _w
PRM_W = _n
CST = {}
_n = 0
for _name, _w in [("ident", 128), ("flip", 128), ("mean_d", 128), ("mean_dv", 128), ("iota", 16), ("seen", 2)]:
    CST[_name] = _n
    _n += _w
CST_W = _n


class Steps:

    def __init__(self, eng, sem):
        self.eng, self.sem, self.n, self.at = eng, sem, 0, None

    def __call__(self, ins):
        ins.then_inc(self.sem, 1)
        self.n += 1

    def join(self):
        self.eng.wait_ge(self.sem, self.n if self.at is None else self.at + (self.n - self.n0))

    def body(self, i, first, each):
        self.n0, self.each = self.n, each
        self.at = (i - first) * each + self.n

    def left(self, iterations):
        assert self.n - self.n0 == self.each, (self.n - self.n0, self.each)
        self.n = self.n0 + iterations * self.each
        self.at = None


def program(nc, a, out):
    f32, u32, bf16 = mybir.dt.float32, mybir.dt.uint32, mybir.dt.bfloat16
    ALU, ACT, AX = mybir.AluOpType, mybir.ActivationFunctionType, mybir.AxisListType
    X = AX.X
    ctx = ExitStack()
    with ctx:
        def sb(name, shape, dt=f32):
            return ctx.enter_context(nc.sbuf_tensor(name, shape, dt))

        def sem(name):
            return ctx.enter_context(nc.semaphore(name))

        wring = sb("wring", [128, RING, SLOT])
        xT = sb("xT", [128, KT, S])
        hT = sb("hT", [128, KT, S])
        cst = sb("cst", [128, CST_W])
        prm = sb("prm", [128, PRM_W])
        memk = sb("memk", [128, 2, 2, S])
        memv = sb("memv", [128, 2, TT, 256])
        zero = sb("zero", [128, 512], bf16)
        eps = sb("eps", [128, 1])
        AW = 31900
        arena = sb("arena", [128, AW])
        free = {"at": 0}

        def phase(at=0):
            free["at"] = at

        def take(*shape, rows=128):
            n = 1
            for d in shape:
                n *= d
            o = free["at"]
            free["at"] += n
            assert free["at"] <= AW, free["at"]
            v = arena[0:rows, o:o + n]
            if len(shape) == 2:
                v = v.rearrange("p (a b) -> p a b", b=shape[1])
            if len(shape) == 3:
                v = v.rearrange("p (a b c) -> p a b c", b=shape[1], c=shape[2])
            if len(shape) == 4:
                v = v.rearrange("p (a b c d) -> p a b c d", b=shape[1], c=shape[2], d=shape[3])
            return v

        def C(name, w, rows=128):
            return cst[0:rows, CST[name]:CST[name] + w]

        def P(name, i=0, w=1, rows=128):
            return prm[0:rows, PRM[name] + i:PRM[name] + i + w]

        ident = C("ident", 128)

        phase()
        sq = take(KT, S)
        memT = take(KT, S)
        memn = [take(KT, S), take(KT, S)]
        sqm = take(KT, S)
        invcnt = take(4, S)
        zp = [take(4, 16 + S) for _ in range(3)]
        pooled = take(4, S)
        poolT = take(4, S)
        zc = take(12, S)
        cu = take(4, 2 + S)
        cy = take(4, S)
        convT = take(4, S)
        zg = take(16, S)
        mixtmp = take(2, 2, S)
        onehots = take(896, rows=33)
        tb = take(896, rows=12)
        mT = zc[:, 0:KT, :]

        phase(4 * KT * S)
        scores = take(UNITS, 2 * NKEYS)
        G = take(NBUF, 2 * D)
        diag = take(2, 4, 128)
        sc = [take(2, 128), take(2, 128)]
        wk = take(2, 128)
        tv = take(2, 16)
        ti = take(2, 16).bitcast(u32)
        tif = take(2, 16)
        cand = take(16, 16)
        cw = take(16, 16)
        fs = [take(16), take(16)]
        pos = take(16).bitcast(u32)
        pij = take(2, 16).bitcast(u32)
        onehot = take(2, 16 * 16)
        eij = take(2, 16)
        idx = [take(16).bitcast(u32), take(16).bitcast(u32)]
        negm = [take(1), take(1)]
        gexp = [take(16), take(16)]
        gsum = [take(1), take(1)]
        ginv = take(1)
        gate = [take(16), take(16)]
        dot = [take(16), take(16)]
        act4 = [take(4), take(4)]
        wv = [take(16), take(16)]
        qTa = arena[:, 0:16 * S].rearrange("p (a b) -> p a b", b=S)
        peer_o = arena[:, 0:TT * D].rearrange("p (a b) -> p a b", b=D)

        phase()
        sqC = take(KT, S)
        gq = take(GH, S, rows=DK)
        gk = take(GH, S, rows=DK)
        gg = take(2 * GH, S, rows=DK)
        gmq = take(2, S)
        glr = take(S, rows=16)
        gv = take(TT, GH * DV)
        reset = take(2, GH * S, rows=DK)
        xg = take(GH, S, rows=DK)
        ge = take(GH, S, rows=DK)
        cs = [take(GH, S, rows=DK) for _ in range(2)]
        dec = [take(GH, S, rows=DK) for _ in range(3)]
        qe = [take(GH, S, rows=DK) for _ in range(2)]
        ke = [take(GH, S, rows=DK) for _ in range(2)]
        lvmask = take(LEVELS - 2, 128)
        pairs = take(4, GH, 128)
        moT = take(2, S)
        attE = take(2, 2, S)
        attP = take(2, 4, 128)
        attm = take(2, 2)
        atts = take(2, 2)
        attr = take(2, 2)
        gout = sqC[0:DK]

        phase(AW - KT * S)
        sqF = take(KT, S)
        phase()
        fy = take(2, 2, S)
        fsa = take(2, S)
        fh = take(2, S)

        phase()
        sqE = take(KT, S)
        xn1 = take(KT, S)
        biasT = take(12, S)
        hank = take(12, S)
        biasC = take(12, S, rows=NC)
        kvc = take(2, 2, S)
        ksw = take(2, 2, S)
        vsw = take(2, TT, 256)
        nq = take(6, S)
        nmq = take(2, S)
        ngl = take(TT, 36)
        kcT = take(2, NC)
        vc = take(256, rows=NC)
        hid = take(2, 60)
        cE = take(TT, 12 * NC)
        cm = take(TT, 12)
        csum = take(TT, 12)
        cr = take(TT, 12)
        gcmp = take(TT, 12)
        nm = take(2, 2)
        ns = take(2, 2)
        nr = take(2, 2)
        places = take(2, 2, LH, 30)
        turned_places = take(2, LH, 30)
        w1_at = free["at"]
        w1 = take(2, LH, 128)
        phase(w1_at)
        pcT = take(TT, 12, 128, rows=NC)
        naT = take(6, S)
        moT1 = take(2, S)
        nE = take(2, 2, S)
        nP = take(2, 4, 128)

        bank = [ctx.enter_context(nc.psum_tensor(f"bank{b}", [128, 512], f32)) for b in range(4)]
        wide = ctx.enter_context(nc.psum_tensor("wide", [128, 4, 512], f32))

        x_in = sem("x_in")
        loaded = sem("loaded")
        more_in = sem("more_in")
        late = sem("late")
        w_full = [sem(f"w_full{r}") for r in range(RING)]
        group_full = sem("group_full")
        freed = {ACT_: sem("freed_by_act"), DVE_: sem("freed_by_dve")}
        zeroed = sem("zeroed")
        fence = {e: sem(f"fence_{e}") for e in ("pool", "dve")}
        squared = sem("squared")
        rooted = sem("rooted")
        normed = sem("normed")
        sact, sdve = sem("act_steps"), sem("dve_steps")
        pool_done, conv_done = sem("pool_done"), sem("conv_done")
        mixed = sem("mixed")
        added = sem("added")
        h2_ready = sem("h2_ready")
        sc_ready, idx_ready, fs_ready, gexp_ready = sem("sc_ready"), sem("idx_ready"), sem("fs_ready"), sem("gexp_ready")
        g_full = [sem(f"g_full{b}") for b in range(NBUF)]
        dots, gelu, wts, diags, v_used = sem("dots"), sem("gelu"), sem("wts"), sem("diags"), sem("v_used")
        peer_sum, peer_out = sem("peer_sum"), sem("peer_out")
        onehot_in, bias_dram = sem("onehot_in"), sem("bias_dram")
        g_turn, g_l, g_cs, g_dif, g_exp, g_qk, g_done, g_sq, g_out = [sem(n) for n in (
            "gla_pairs_used", "gate_logs", "gate_sums", "gla_to_middle", "gla_decay", "gla_decayed", "gla_summed", "gla_squared", "gla_out")]
        a_s, a_m, a_e, a_p, a_t, a_c, a_o, a_done = [sem(n) for n in (
            "att_scores", "att_max", "att_exp", "att_probs", "att_turned", "att_probsT", "att_sum", "att_out")]
        f_lin, f_conv, f_silu, f_hid, f_down, f_sum = [sem(n) for n in (
            "ffn_lin", "ffn_conv", "ffn_silu", "ffn_hidden", "ffn_down", "ffn_summed")]
        c_pos, c_turn, c_moved, c_e, c_x, c_p = [sem(n) for n in (
            "cmp_windows", "cmp_turned_windows", "cmp_windows_moved", "cmp_shifted", "cmp_exp", "cmp_probs")]
        stored = sem("stored")

        JOBS = [(0, "mem", h, 1) for h in range(4)]
        JOBS += [(1, "mem", h, 1) for h in range(4)]
        JOBS += [(1, "nsa", h, tt) for tt in range(TT) for h in range(12)]
        JOBS0, JOBS1, JOBS2 = range(0, 4), range(4, 8), range(8, len(JOBS))

        def job_bufs(layer):
            return (attE, attP, attm, atts, attr, moT, gmq) if layer == 0 else (nE, nP, nm, ns, nr, moT1, nmq)

        block = ctx.enter_context(nc.Block())

        @block.sync
        def _(sp):
            sp.dma_start(xT[:], a["xT"]).then_inc(x_in, 16)
            sp.dma_start(cst[:], a["cst"]).then_inc(loaded, 16)
            sp.dma_start(prm[:], a["prm"]).then_inc(loaded, 16)
            for name, slots, width in STREAM:
                n0 = SLOT0[name]

                def load(slot, s, more=0):
                    if n0 + s >= RING:
                        kind, count = USED[n0 + s - RING]
                        sp.wait_ge(group_full if kind == "group" else f_down, more + count)
                    sp.dma_start(wring[:, (n0 + s) % RING, 0:width], a[name][slot]).then_inc(w_full[(n0 + s) % RING], 16)

                rounds = (slots - RING) // RING if slots >= 3 * RING else 0
                for s in range(RING if rounds else 0):
                    load(s, s)
                if name == "win":
                    sp.dma_start(memT, a["memT"]).then_inc(more_in, 16)
                    sp.dma_start(invcnt, a["invcnt"]).then_inc(more_in, 16)
                if rounds:
                    with sp.Fori(0, rounds) as i:
                        for s in range(RING, 2 * RING):
                            load(i * RING + s, s, i * RING)
                for s in range(RING * (rounds + 1) if rounds else 0, slots):
                    load(s, s)
            for n in range(4):
                sp.wait_ge(normed, 8 * 10 + 2 * n + 2)
                sp.dma_start(out[:, 2 * n:2 * n + 2, :], hT[:, 2 * n:2 * n + 2, :]).then_inc(stored, 16)
            sp.wait_ge(stored, 64)

        @block.gpsimd
        def _(pool):
            def gather(par, u, first):
                pool.wait_ge(idx_ready, u + 1)
                pool.sem_inc(fence["pool"])
                for s in range(TOPK):
                    b = s % NBUF
                    if not (first and s < NBUF):
                        pool.wait_ge(v_used, 16 * u + (s - NBUF + 1))
                        pool.sem_inc(fence["pool"])
                    pool.indirect_dma_start(out=G[:, b, :], out_offset=None, in_=a["uv"],
                                            in_offset=bass.IndirectOffsetOnAxis(ap=idx[par][:, s:s + 1], axis=0),
                                            bounds_check=NKEYS * NKEYS - 1, oob_is_err=True).then_inc(g_full[b], 16)

            rows = a["rows"].tensor
            pool.dma_start(onehots, a["onehot"]).then_inc(onehot_in, 16)
            pool.wait_ge(freed[ACT_], 2)
            pool.dma_start(a["rows"], tb).then_inc(bias_dram, 16)
            pool.wait_ge(bias_dram, 16)
            pool.wait_ge(normed, 32)
            gather(0, 0, True)
            gather(1, 1, False)
            with pool.Fori(1, UNITS // 2) as i:
                gather(0, 2 * i, False)
                gather(1, 2 * i + 1, False)
            pool.wait_ge(normed, 40)
            pool.dma_start(reset, a["reset"]).then_inc(late, 16)
            pool.dma_start(lvmask, a["lvmask"]).then_inc(late, 16)
            for n in range(LEVELS - 1):
                m = 1 << n
                pool.wait_ge(g_cs, 1 if m <= 8 else 2)
                if n >= 3:
                    pool.wait_ge(g_qk, n - 1)
                c = cs[0 if m <= 8 else 1].rearrange("p h (c j) -> p (h c) j", j=2 * m)
                nc.gpsimd.tensor_tensor(dec[n % 3].rearrange("p h (c j) -> p (h c) j", j=2 * m), c,
                                        c[:, :, m - 1:m].broadcast_to([DK, GH * S // (2 * m), 2 * m]), ALU.subtract)\
                    .then_inc(g_dif, 1)
            pool.wait_ge(added, 12)
            pool.dma_start(w1, a["w1"]).then_inc(late, 16)
            pool.dma_start(hank, bass.AP(rows, 512, [[1, 128], [896, 12], [1, S]])).then_inc(late, 16)
            pool.dma_start(biasC, bass.AP(rows, 0, [[16, NC], [896, 12], [1, S]])).then_inc(late, 16)
            pool.wait_ge(c_turn, 8)
            pool.dma_start(places[64:128, 0], turned_places[0:64]).then_inc(c_moved, 16)
            pool.dma_start(places[0:64, 1], turned_places[64:128]).then_inc(c_moved, 16)

        @block.scalar
        def _(act):
            steps = Steps(act, sact)

            def copy(o, i, scale=1.0, func=ACT.Copy, bias=None):
                kw = {"bias": bias} if bias is not None else {}
                return nc.scalar.activation(o, i, func, scale=scale, **kw)

            def full(stage, i=0):
                act.wait_ge(group_full, GROUP0[stage] + i + 1)
                return bank[(GROUP0[stage] + i) % 4]

            def halves(b, rows=128):
                return b[0:rows, :].rearrange("p (a t) -> p a t", a=2)

            def square(o, i, wait, at):
                for n in range(4):
                    act.wait_ge(wait, at[n])
                    copy(o[:, 2 * n:2 * n + 2, :], i[:, 2 * n:2 * n + 2, :], func=ACT.Square).then_inc(squared, 1)

            def root(stage, i=0, rows=128, n=S):
                b = full(stage, i)[0:rows, 0:n]
                copy(b, b, func=ACT.Sqrt, bias=eps[0:rows]).then_inc(rooted, 1)

            square(sq, xT, x_in, [16] * 4)
            for i in range(2):
                n = 512 if i == 0 else 384
                copy(tb[:, 512 * i:512 * i + n], full("bias", i)[0:12, 0:n])\
                    .then_inc(freed[ACT_], 1)
            act.wait_ge(zeroed, 6)
            root("mean_x")
            square(sqm, memT, more_in, [32] * 4)
            for i in range(8):
                b = full("win", i)
                if i == 0:
                    act.wait_ge(zeroed, 4)
                dst = zp[0][:, 2 * i:2 * i + 2, 16:16 + S] if i < 2 else zc[:, 2 * i - 4:2 * i - 2, :]
                copy(dst, halves(b)).then_inc(freed[ACT_], 1)
            with act.Fori(2, 4) as i:
                for s in range(4):
                    act.wait_ge(group_full, i * 4 + (GROUP0["win"] + s + 1))
                    copy(zg[:, bass.ds(i * 8 + (2 * s - 16), 2), :], halves(bank[(GROUP0["win"] + s) % 4]),
                         func=ACT.Sigmoid).then_inc(freed[ACT_], 1)
            for i in range(2):
                b = full("poolmap", i)
                for j in range(2):
                    ins = copy(poolT[:, 2 * i + j, :], b[:, j * S:(j + 1) * S], scale=P("pool_scale", 2 * i + j))
                ins.then_inc(freed[ACT_], 1)
            square(sq, xT, added, [1, 2, 3, 4])
            root("mean_ffn")
            root("mean_mem")
            def queries(i, b):
                copy(qTa[:, 2 * i:2 * i + 2, :], halves(b)).then_inc(freed[ACT_], 1)

            def exps(par, u):
                act.wait_ge(fs_ready, u + 1)
                nc.scalar.activation(gexp[par], fs[par], ACT.Exp, bias=negm[par],
                                     accum_out=gsum[par]).then_inc(gexp_ready, 1)

            for i in range(2):
                queries(i, full("wqa", i))
            copy(scores[:, 0:2, :], halves(full("scores_a"))).then_inc(freed[ACT_], 1)
            act.wait_ge(freed[ACT_], TAKEN[GROUP0["scores_a"]])
            for par in range(2):
                copy(sc[par], scores[:, par, :].rearrange("p (a b) -> p a b", a=2)).then_inc(sc_ready, 1)
            for i in range(4):
                queries(i + 2, full("wq", i))
            exps(0, 0)
            for i in range(4, 6):
                queries(i + 2, full("wq", i))
            for i in range(7):
                copy(scores[:, 2 * i + 2:2 * i + 4, :], halves(full("scores", i))).then_inc(freed[ACT_], 1)
            act.wait_ge(freed[ACT_], TAKEN[GROUP0["scores"] + 6])

            def memory():
                for l in range(2):
                    copy(memk[:, l], halves(full("memkv", 2 * l))).then_inc(freed[ACT_], 1)
                    copy(memv[:, l], halves(full("memkv", 2 * l + 1))).then_inc(freed[ACT_], 1)

            def unit(par, u, first, last, between=False):
                if not last and not (first and par == 0):
                    act.wait_ge(idx_ready, u + 1)
                    nxt = scores[:, u + 1, :] if isinstance(u, int) else scores[:, bass.ds(u + 1, 1), :].rearrange(
                        "p o n -> p (o n)")
                    copy(sc[1 - par].rearrange("p a b -> p (a b)"), nxt).then_inc(sc_ready, 1)
                if not first:
                    exps(par, u)
                if between:
                    memory()
                for q in range(4):
                    act.wait_ge(dots, u * 16 + (4 * q + 4))
                    copy(act4[q % 2], dot[par][:, 4 * q:4 * q + 4], func=ACT.Gelu).then_inc(gelu, 1)
                    act.wait_ge(wts, u * 4 + (q + 1))
                    if not (first and q < 2):
                        act.wait_ge(v_used, u * 16 + (4 * q - 4))
                    for e in range(4):
                        ins = copy(diag[:, q % 2, e, :], ident, scale=wv[par][:, 4 * q + e:4 * q + e + 1])
                    ins.then_inc(diags, 1)

            unit(0, 0, True, False)
            unit(1, 1, False, False)
            with act.Fori(1, HEADS // 2) as i:
                unit(0, 2 * i, False, False)
                unit(1, 2 * i + 1, False, False)
            unit(0, HEADS, False, False, between=True)
            unit(1, HEADS + 1, False, False)
            with act.Fori(HEADS // 2 + 1, UNITS // 2 - 1) as i:
                unit(0, 2 * i, False, False)
                unit(1, 2 * i + 1, False, False)
            unit(0, UNITS - 2, False, False)
            unit(1, UNITS - 1, False, True)

            square(memn[0], xT, added, [6, 6, 8, 8])
            root("mean_fin")
            square(sqC, xT, normed, [34, 36, 38, 40])
            root("mean_mix0")
            for i in range(14):
                b = full("gla_in", i)
                if i < 2:
                    ins = copy(gq[:, 2 * i:2 * i + 2, :], halves(b, DK), scale=float(DK) ** -0.5)
                elif i < 4:
                    ins = copy(gk[:, 2 * i - 4:2 * i - 2, :], halves(b, DK))
                elif i < 8:
                    ins = copy(gg[:, 2 * i - 8:2 * i - 6, :], halves(b, DK), func=ACT.Silu)
                elif i == 8:
                    ins = copy(gmq, halves(b), scale=0.125)
                elif i == 9:
                    ins = copy(glr, b[0:16, 0:S])
                else:
                    c, t = divmod(i - 10, 2)
                    ins = copy(gv[:, t, 384 * c:384 * c + 384], b[:, 0:384])
                ins.then_inc(freed[ACT_], 1)
            for h in range(GH):
                b = full("gla_gate", h // 2)
                ins = copy(xg[:, h, :], b[0:DK, (h % 2) * S:(h % 2 + 1) * S], func=ACT.Identity, bias=P("b_gate", h, rows=DK))
                if h % 2:
                    ins.then_inc(freed[ACT_], 1)
                else:
                    steps(ins)
            steps.join()
            act.wait_ge(freed[ACT_], TAKEN[GROUP0["gla_gate"] + 1])
            steps(copy(ge, xg, func=ACT.Abs))
            steps.join()
            steps(copy(ge, ge, func=ACT.Exp, scale=-1.0))
            steps.join()
            copy(ge, ge, func=ACT.Ln, bias=1.0).then_inc(g_l, 1)
            for n in range(LEVELS - 1):
                act.wait_ge(g_dif, n + 1)
                steps(copy(dec[n % 3], dec[n % 3], func=ACT.Abs))
                steps.join()
                copy(dec[n % 3], dec[n % 3], func=ACT.Exp, scale=-1.0 / 16).then_inc(g_exp, 1)
            act.wait_ge(g_done, 1)
            for n in range(2):
                copy(sqC[0:DK, 4 * n:4 * n + 4, :], wide[0:DK, 2 * n:2 * n + 2, :].rearrange("p a (b t) -> p (a b) t", b=2),
                     func=ACT.Square).then_inc(g_sq, 1)
            for i in range(2):
                root("gla_ms", i, DK, 2 * S)

            def expo(J):
                layer, kind, h, tt = JOBS[J]
                E, _, m, s_, _, _, _ = job_bufs(layer)
                w = S if kind == "mem" else 128 * (tt + 1)
                act.wait_ge(a_m, J + 1)
                for j in range(2):
                    src = wide[:, J % 2, j * S:j * S + w] if kind == "mem" else E[:, J % 2, j, 0:w]
                    if j == 0 and J - 2 >= (0 if layer == 0 else JOBS1.start):
                        act.wait_ge(a_t, J - 1)
                    ins = nc.scalar.activation(E[:, J % 2, j, 0:w], src, ACT.Exp, bias=m[:, J % 2, j:j + 1],
                                               accum_out=s_[:, J % 2, j:j + 1])
                ins.then_inc(a_e, 1)

            def outs(J):
                layer, kind, h, tt = JOBS[J]
                _, Pt, _, _, _, mo, _ = job_bufs(layer)
                blocks = 4 if kind == "mem" or tt == 1 else 2
                act.wait_ge(a_t, J + 1)
                copy(Pt[:, J % 2, 0:blocks, :], wide[:, 2, 0:blocks * 128].rearrange("p (a b) -> p a b", b=128)).then_inc(a_c, 1)
                act.wait_ge(a_o, J + 1)
                cols = slice(tt * 128, tt * 128 + 128)
                if kind == "mem":
                    lo = 64 * (h % 2)
                    copy(mo[lo:lo + 64, h // 2, :], wide[lo:lo + 64, 3, 0:S]).then_inc(a_done, 1)
                else:
                    g, r = divmod(h, 3)
                    lo = 64 * (g % 2)
                    copy(naT[lo:lo + 64, (g // 2) * 3 + r, cols], wide[lo:lo + 64, 3, 0:128]).then_inc(a_done, 1)

            def attend(jobs):
                expo(jobs[0])
                expo(jobs[1])
                for J in jobs:
                    outs(J)
                    if J + 2 in jobs:
                        expo(J + 2)

            act.wait_ge(g_out, 1)
            attend(JOBS0)

            def ffn(stage, layer):
                steps.join()
                g0, k0 = GROUP0[stage], layer * FT

                def lin(j, k):
                    act.wait_ge(group_full, j + (g0 + 1))
                    if not isinstance(j, int) or j >= 2 or layer:
                        act.wait_ge(f_hid, j + (k0 - 1))
                    b = bank[(g0 + k) % 4]
                    wcol = PRM["ffn_w"] + layer * 132
                    bcol = PRM["ffn_b"] + layer * 44
                    for c in range(2):
                        if isinstance(j, int):
                            o = c * FT + j
                            w2_, b_ = prm[:, wcol + 3 * o + 2:wcol + 3 * o + 3], prm[:, bcol + o:bcol + o + 1]
                        else:
                            w2_ = prm[:, bass.ds(j * 3 + (wcol + 3 * c * FT + 2), 1)]
                            b_ = prm[:, bass.ds(j + (bcol + c * FT), 1)]
                        ins = copy(fy[:, k % 2, c, :], b[:, c * S:(c + 1) * S], func=ACT.Identity, scale=w2_, bias=b_)
                    ins.then_inc(f_lin, 1)

                def silu(j, k):
                    act.wait_ge(f_conv, j + (k0 + 1))
                    copy(fsa[:, k % 2, :], fy[:, k % 2, 0, :], func=ACT.Silu).then_inc(f_silu, 1)

                for j in range(2):
                    lin(j, j)
                    silu(j, j)
                with act.Fori(0, (FT - 2) // 4) as i:
                    for s in range(4):
                        lin(i * 4 + (s + 2), s + 2)
                        silu(i * 4 + (s + 2), s + 2)

            square(sqF, xT, added, [9, 10, 11, 12])
            root("mean_f0")
            ffn("ffn0", 0)
            square(sqE, xT, added, [13, 14, 15, 16])
            root("mean_kv")
            for n in range(6):
                copy(biasT[:, 2 * n:2 * n + 2, :], halves(full("flip", n))).then_inc(freed[ACT_], 1)
            for i in range(6):
                b = halves(full("kv", i))
                dst = kvc[:, i] if i < 2 else ksw[:, i - 2] if i < 4 else vsw[:, i - 4]
                copy(dst, b).then_inc(freed[ACT_], 1)
            for i in range(3):
                copy(nq[:, 2 * i:2 * i + 2, :], halves(full("nsaq", i)), scale=0.125).then_inc(freed[ACT_], 1)
            b = full("cmp_hid")
            for kind in range(2):
                ins = copy(hid[:, kind, :], b[:, 60 * kind:60 * kind + 60], func=ACT.Silu, bias=P("cmp_b1", kind))
            ins.then_inc(freed[ACT_], 1)
            copy(nmq, halves(full("nsamq")), scale=0.125).then_inc(freed[ACT_], 1)
            copy(ngl, full("nsagl")[:, 0:72].rearrange("p (t g) -> p t g", t=TT), func=ACT.Sigmoid).then_inc(freed[ACT_], 1)
            for t in range(TT):
                act.wait_ge(c_e, 2 * t + 2)
                copy(cE[:, t, :], cE[:, t, :], func=ACT.Exp).then_inc(c_x, 1)
            attend(JOBS1)
            for n in range(6):
                t, c = divmod(n, 3)
                copy(pcT[:, t, 4 * c:4 * c + 4, :], full("cmp_pT", n)[0:NC, :].rearrange("p (h q) -> p h q", h=4))\
                    .then_inc(freed[ACT_], 1)
            attend(JOBS2)
            square(sqF, xT, added, [17, 18, 19, 20])
            root("mean_f1")
            ffn("ffn1", 1)
            square(sqF, xT, added, [21, 22, 23, 24])
            root("mean_out")

        @block.vector
        def _(dve):
            steps = Steps(dve, sdve)
            V = nc.vector

            def full(stage, i=0):
                dve.wait_ge(group_full, GROUP0[stage] + i + 1)
                return bank[(GROUP0[stage] + i) % 4]

            def halves(b, rows=128):
                return b[0:rows, :].rearrange("p (a t) -> p a t", a=2)

            def norm(stage, src, outs):
                b = full(stage)
                norm.n += 1
                dve.wait_ge(rooted, norm.n)
                steps(V.reciprocal(b[:, 0:S], b[:, 0:S]))
                steps.join()
                for dst, gain, col in outs:
                    for k in range(KT):
                        V.scalar_tensor_tensor(out=dst[:, k, :], in0=src[:, k, :], scalar=P(gain, col + k), in1=b[:, 0:S],
                                               op0=ALU.mult, op1=ALU.mult).then_inc(normed, 1)
                dve.drain().then_inc(freed[DVE_], 1)

            norm.n = 0
            V.memset(zero[:], 0.0).then_inc(zeroed, 1)
            for z in zp:
                V.memset(z[:, :, 0:16], 0.0).then_inc(zeroed, 1)
            V.memset(cu[:, :, 0:2], 0.0).then_inc(zeroed, 1)
            V.memset(eps[:], EPS).then_inc(zeroed, 1)
            dve.wait_ge(x_in, 16)
            dve.wait_ge(loaded, 32)
            norm("mean_x", xT, [(hT, "g_mix", 0)])
            dve.wait_ge(freed[ACT_], TAKEN[GROUP0["win"] + 1])
            dve.wait_ge(zeroed, 5)
            dve.wait_ge(more_in, 32)
            src = zp[0]
            for g in range(4):
                dst = zp[1 + g % 2]
                sh = 1 << g
                steps(V.tensor_tensor(dst[:, g:4, 16:16 + S], src[:, g:4, 16:16 + S], src[:, g:4, 16 - sh:16 - sh + S], ALU.add))
                steps.join()
                steps(V.tensor_tensor(pooled[:, g, :], dst[:, g, 16:16 + S], invcnt[:, g, :], ALU.mult))
                steps.join()
                src = dst
            V.tensor_tensor(pooled, pooled, zp[0][:, :, 16:16 + S], ALU.subtract).then_inc(pool_done, 1)
            dve.wait_ge(freed[ACT_], TAKEN[GROUP0["win"] + 7])
            steps(V.tensor_tensor(cu[:, :, 2:2 + S], zc[:, 0:4, :], zc[:, 8:12, :], ALU.mult))
            steps.join()
            for t in range(4):
                steps(V.tensor_scalar(cy[:, t, :], cu[:, t, 2:2 + S], P("conv_w", 3 * t + 2), None, ALU.mult))
            steps.join()
            for tap in (1, 0):
                for t in range(4):
                    steps(V.scalar_tensor_tensor(out=cy[:, t, :], in0=cu[:, t, tap:tap + S], scalar=P("conv_w", 3 * t + tap),
                                                 in1=cy[:, t, :], op0=ALU.mult, op1=ALU.add))
                steps.join()
            V.tensor_tensor(convT, cy, zc[:, 4:8, :], ALU.mult).then_inc(conv_done, 1)
            dve.wait_ge(freed[ACT_], TAKEN[GROUP0["poolmap"] + 1])
            dve.wait_ge(conv_done, 1)
            for m in range(KT):
                b = full("mix", m)
                if m >= 2:
                    dve.wait_ge(mixed, m - 1)
                V.tensor_tensor(mixtmp[:, m % 2], halves(b), zg.rearrange("p (g k) t -> p g k t", g=2)[:, :, m, :],
                                ALU.mult).then_inc(freed[DVE_], 1)
                dve.wait_ge(freed[DVE_], TAKEN[GROUP0["mix"] + m])
                V.tensor_tensor(mT[:, m, :], mixtmp[:, m % 2, 0, :], mixtmp[:, m % 2, 1, :], ALU.add).then_inc(mixed, 1)

            def add_groups(stage):
                for i in range(4):
                    b = full(stage, i)
                    V.tensor_tensor(xT[:, 2 * i:2 * i + 2, :], halves(b), xT[:, 2 * i:2 * i + 2, :], ALU.add)\
                        .then_inc(added, 1)
                    add_groups.n += 1
                    dve.drain().then_inc(freed[DVE_], 1)
            add_groups.n = 0

            add_groups("wout")
            norm("mean_ffn", xT, [(hT, "g_ffn", 0)])
            norm("mean_mem", memT, [(memn[0], "norm_mem", 0), (memn[1], "norm_mem", 8)])

            def join():
                steps.join()
                dve.sem_inc(fence["dve"])

            def topk16(vals, ixs, src, work, n):
                for p in range(n):
                    steps(V.max(vals[p][:, 0:8], src[p]))
                join()
                for p in range(n):
                    steps(V.max_index(ixs[p][:, 0:8], vals[p][:, 0:8], src[p]))
                    steps(V.match_replace(work[p], vals[p][:, 0:8], src[p], -3.0e38))
                join()
                for p in range(n):
                    steps(V.max(vals[p][:, 8:16], work[p]))
                join()
                for p in range(n):
                    steps(V.max_index(ixs[p][:, 8:16], vals[p][:, 8:16], work[p]))
                steps.join()

            def select(par, u):
                dve.wait_ge(sc_ready, u + 1)
                dve.sem_inc(fence["dve"])
                topk16([tv[:, p, :] for p in range(2)], [ti[:, p, :] for p in range(2)],
                       [sc[par][:, p, :] for p in range(2)], [wk[:, p, :] for p in range(2)], 2)
                steps(V.tensor_copy(tif, ti))
                steps(V.tensor_tensor(cand, tv[:, 0, :].unsqueeze(2).broadcast_to([128, 16, 16]),
                                      tv[:, 1, :].unsqueeze(1).broadcast_to([128, 16, 16]), ALU.add))
                join()
                flat = cand.rearrange("p a b -> p (a b)")
                topk16([fs[par]], [pos], [flat], [cw.rearrange("p a b -> p (a b)")], 1)
                V.tensor_scalar(negm[par], fs[par][:, 0:1], -1.0, None, ALU.mult).then_inc(fs_ready, 1)
                steps(V.tensor_scalar(pij[:, 0, :], pos, 4, 15, ALU.logical_shift_right, ALU.bitwise_and))
                steps(V.tensor_scalar(pij[:, 1, :], pos, 15, 15, ALU.bitwise_and, ALU.bitwise_and))
                steps.join()
                for p in range(2):
                    oh = onehot[:, p, :].rearrange("p (k i) -> p k i", k=16)
                    steps(V.tensor_tensor(oh, pij[:, p, :].unsqueeze(2).broadcast_to([128, 16, 16]),
                                          C("iota", 16).unsqueeze(1).broadcast_to([128, 16, 16]), ALU.is_equal))
                steps.join()
                for p in range(2):
                    oh = onehot[:, p, :].rearrange("p (k i) -> p k i", k=16)
                    steps(V.tensor_tensor(oh, oh, tif[:, p, :].unsqueeze(1).broadcast_to([128, 16, 16]), ALU.mult))
                steps.join()
                steps(V.tensor_reduce(eij.rearrange("p a b -> p (a b)"), onehot.rearrange("p a (k i) -> p (a k) i", k=16),
                                      X, ALU.add))
                steps.join()
                V.scalar_tensor_tensor(out=idx[par], in0=eij[:, 0, :], scalar=float(NKEYS), in1=eij[:, 1, :],
                                       op0=ALU.mult, op1=ALU.add).then_inc(idx_ready, 1)
            SELECT = 2 + 4 + 2 + 2 + 2 + 1 + 2 + 1 + 1 + 2 + 2 + 2 + 1

            def weigh(par, u, tt):
                dve.wait_ge(gexp_ready, u + 1)
                steps(V.reciprocal(ginv, gsum[par]))
                steps.join()
                steps(V.tensor_scalar(gate[par], gexp[par], ginv, None, ALU.mult))
                steps.join()
                for q in range(4):
                    for s in range(4 * q, 4 * q + 4):
                        b = s % NBUF
                        dve.wait_ge(g_full[b], u * 32 + 16 * (s // NBUF + 1))
                        V.tensor_tensor_reduce(out=G[:, b, 0:D], in0=G[:, b, 0:D],
                                               in1=wide[:, 2 * tt:2 * tt + 2, :].rearrange("p a b -> p (a b)"),
                                               scale=1.0, scalar=0.0, op0=ALU.mult, op1=ALU.add,
                                               accum_out=dot[par][:, s:s + 1]).then_inc(dots, 1)
                    dve.wait_ge(gelu, u * 4 + (q + 1))
                    V.tensor_tensor(wv[par][:, 4 * q:4 * q + 4], act4[q % 2], gate[par][:, 4 * q:4 * q + 4],
                                    ALU.mult).then_inc(wts, 1)
            WEIGH = 2

            def keep_sum(tt):
                dve.wait_ge(peer_sum, tt + 1)
                steps(V.tensor_copy(peer_o[:, tt, 0:512], bank[0][:]))
                steps.join()
                V.tensor_copy(peer_o[:, tt, 512:1024], bank[1][:]).then_inc(peer_out, 1)

            dve.wait_ge(h2_ready, 1)
            select(0, 0)
            with dve.Fori(0, HEADS // 2) as i:
                steps.body(i, 0, 2 * (SELECT + WEIGH))
                for par in range(2):
                    select(1 - par, 2 * i + (par + 1))
                    weigh(par, 2 * i + par, 0)
                steps.left(HEADS // 2)
            keep_sum(0)
            with dve.Fori(HEADS // 2, HEADS - 1) as i:
                steps.body(i, HEADS // 2, 2 * (SELECT + WEIGH))
                for par in range(2):
                    select(1 - par, 2 * i + (par + 1))
                    weigh(par, 2 * i + par, 1)
                steps.left(HEADS // 2 - 1)
            select(1, UNITS - 1)
            weigh(0, UNITS - 2, 1)
            weigh(1, UNITS - 1, 1)
            keep_sum(1)
            for n in range(4):
                k, t = divmod(n, 2)
                b = full("peer_back", n)
                o = xT[:, 4 * k:4 * k + 4, t * 128:t * 128 + 128]
                V.tensor_tensor(o, b[:].rearrange("p (k q) -> p k q", k=4), o, ALU.add).then_inc(added, 1)
                add_groups.n += 1
                dve.drain().then_inc(freed[DVE_], 1)
            norm("mean_fin", xT, [(xT, "g_final", 0)])
            dve.wait_ge(normed, 40)
            norm("mean_mix0", xT, [(hT, "norm_mix", 0)])

            dve.wait_ge(g_l, 1)
            dve.wait_ge(late, 32)
            steps(V.scalar_tensor_tensor(out=xg, in0=xg, scalar=0.0, in1=ge, op0=ALU.min, op1=ALU.subtract))
            steps.join()
            for n in range(2):
                V.tensor_tensor_scan(cs[n].rearrange("p h t -> p (h t)"), reset[:, n, :], xg.rearrange("p h t -> p (h t)"),
                                     0.0, ALU.mult, ALU.add).then_inc(g_cs, 1)

            def decayed(n):
                if n >= 2:
                    dve.wait_ge(group_full, GROUP0["gla_pair"] + 2 * n)
                dve.wait_ge(g_exp, n + 1)
                V.tensor_tensor(qe[n % 2], gq, dec[n % 3], ALU.mult)
                V.tensor_tensor(ke[n % 2], gk, dec[n % 3], ALU.mult).then_inc(g_qk, 1)

            def keep_pairs(level):
                for t in range(TT if level < LEVELS - 1 else 1):
                    g = 2 * level + t
                    b = full("gla_pair", g)
                    if g >= 4:
                        dve.wait_ge(g_turn, g - 3)
                    bv = b[:].rearrange("p (h q) -> p h q", h=GH)
                    if level == LEVELS - 1:
                        ins = V.tensor_copy(pairs[:, g % 4], bv)
                    else:
                        m = ident if level == 0 else lvmask[:, level - 1, :]
                        ins = V.tensor_tensor(pairs[:, g % 4], bv, m.unsqueeze(1).broadcast_to([128, GH, 128]), ALU.mult)
                    ins.then_inc(freed[DVE_], 1)

            for n in range(LEVELS - 1):
                decayed(n)
                keep_pairs(n)
            keep_pairs(LEVELS - 1)
            for h2 in range(2):
                b = full("gla_ms", h2)
                norm.n += 1
                dve.wait_ge(rooted, norm.n)
                steps(V.reciprocal(b[0:DK, :], b[0:DK, :]))
                steps.join()
                for j in range(2):
                    h = 2 * h2 + j
                    for v in range(2):
                        steps(V.scalar_tensor_tensor(out=gg[:, 2 * h + v, :], in0=gg[:, 2 * h + v, :],
                                                     scalar=P("out_norm", v, rows=DK), in1=b[0:DK, j * S:(j + 1) * S],
                                                     op0=ALU.mult, op1=ALU.mult))
                steps.join()
                dve.drain().then_inc(freed[DVE_], 1)
            V.tensor_tensor(gout, wide[0:DK].rearrange("p a (b t) -> p (a b) t", b=2), gg, ALU.mult).then_inc(g_out, 1)

            def maxi(J):
                layer, kind, h, tt = JOBS[J]
                E, _, m, _, _, _, _ = job_bufs(layer)
                w = S if kind == "mem" else 128 * (tt + 1)
                dve.wait_ge(a_s, J + 1)
                src = wide[:, J % 2, :].rearrange("p (a s) -> p a s", a=2)[:, :, 0:w]
                if J - 2 >= (0 if layer == 0 else JOBS1.start):
                    dve.wait_ge(a_t, J - 1)
                    dve.wait_ge(a_e, J - 1)
                if kind == "nsa":
                    bias = biasT[:, h, S - w:S].unsqueeze(1).broadcast_to([128, 2, w])
                    steps(V.tensor_tensor(E[:, J % 2, :, 0:w], src, bias, ALU.add))
                    steps.join()
                    src = E[:, J % 2, :, 0:w]
                V.tensor_reduce(m[:, J % 2, :], src, X, ALU.max, negate=True).then_inc(a_m, 1)

            def probs(J):
                layer, kind, h, tt = JOBS[J]
                E, _, _, s_, r_, _, _ = job_bufs(layer)
                w = S if kind == "mem" else 128 * (tt + 1)
                dve.wait_ge(a_e, J + 1)
                steps(V.tensor_scalar(r_[:, J % 2, :], s_[:, J % 2, :], 1e-30, None, ALU.max))
                steps.join()
                steps(V.reciprocal(r_[:, J % 2, :], r_[:, J % 2, :]))
                steps.join()
                if kind == "nsa":
                    steps(V.tensor_tensor(r_[:, J % 2, :], r_[:, J % 2, :], ngl[:, tt, 3 * h + 1:3 * h + 3], ALU.mult))
                    steps.join()
                for j in range(2):
                    ins = V.tensor_scalar(E[:, J % 2, j, 0:w], E[:, J % 2, j, 0:w], r_[:, J % 2, j:j + 1], None, ALU.mult)
                ins.then_inc(a_p, 1)

            def attend(jobs):
                maxi(jobs[0])
                maxi(jobs[1])
                probs(jobs[0])
                for J in jobs:
                    if J + 1 in jobs:
                        probs(J + 1)
                    if J + 2 in jobs:
                        maxi(J + 2)

            attend(JOBS0)
            add_groups("wout0")
            norm("mean_f0", xT, [(hT, "norm_ffn", 0)])

            def ffn(stage, layer):
                g0, k0 = GROUP0[stage], layer * FT
                d0 = TAKEN[g0] - 1
                wcol = PRM["ffn_w"] + layer * 132

                def tile(j, k):
                    dve.wait_ge(f_lin, j + (k0 + 1))
                    b = bank[(g0 + k) % 4]
                    for tap in (1, 0):
                        sh = 2 - tap
                        for c in range(2):
                            if isinstance(j, int):
                                o = wcol + 3 * (c * FT + j) + tap
                                w_ = prm[:, o:o + 1]
                            else:
                                w_ = prm[:, bass.ds(j * 3 + (wcol + 3 * c * FT + tap), 1)]
                            ins = V.scalar_tensor_tensor(out=fy[:, k % 2, c, sh:S], in0=b[:, c * S:c * S + S - sh], scalar=w_,
                                                         in1=fy[:, k % 2, c, sh:S], op0=ALU.mult, op1=ALU.add)
                            if tap == 0 and c == 0:
                                ins.then_inc(f_conv, 1)
                            elif tap == 0 and c == 1:
                                ins.then_inc(freed[DVE_], 1)
                            else:
                                steps(ins)
                        if tap:
                            steps.join()
                    dve.wait_ge(f_silu, j + (k0 + 1))
                    dve.wait_ge(freed[DVE_], j + (d0 + 1))
                    if not isinstance(j, int) or j >= 2 or layer:
                        dve.wait_ge(f_down, j + (k0 - 1))
                    V.tensor_tensor(fh[:, k % 2, :], fsa[:, k % 2, :], fy[:, k % 2, 1, :], ALU.mult).then_inc(f_hid, 1)

                for j in range(2):
                    tile(j, j)
                with dve.Fori(0, (FT - 2) // 4) as i:
                    steps.body(i, 0, 8)
                    for s in range(4):
                        tile(i * 4 + (s + 2), s + 2)
                    steps.left((FT - 2) // 4)
                dve.wait_ge(f_sum, layer + 1)
                for n in range(4):
                    V.tensor_tensor(xT[:, 2 * n:2 * n + 2, :], wide[:, n, :].rearrange("p (a t) -> p a t", a=2),
                                    xT[:, 2 * n:2 * n + 2, :], ALU.add).then_inc(added, 1)
                add_groups.n += 4
                dve.wait_ge(added, add_groups.n)

            ffn("ffn0", 0)
            norm("mean_kv", xT, [(hT, "kv_norm", 0), (xn1, "norm_mix", 8)])

            dve.wait_ge(freed[ACT_], TAKEN[GROUP0["kv"] + 1])
            for turned in (True, False):
                for base in range(2):
                    lo, half = 64 * base, 1 - base if turned else base
                    for kind in range(2):
                        for gp in range(2):
                            src = kvc[lo:lo + 64, kind, gp, LH * half:S]
                            win = bass.AP(src.tensor, src.offset, [list(src.ap[0]), [1, LH], [16, NC]])
                            o = PRM["cmp_pos"] + 32 * kind + LH * half
                            ps = prm[lo:lo + 64, o:o + LH].unsqueeze(2).broadcast_to([64, LH, NC])
                            dst = turned_places[lo:lo + 64, kind] if turned else places[lo:lo + 64, base, kind]
                            V.tensor_tensor(dst[:, :, gp * NC:(gp + 1) * NC], win, ps, ALU.add)\
                                .then_inc(c_turn if turned else c_pos, 1)
            b = full("cmp_out")
            for base in range(2):
                lo = 64 * base
                steps(V.tensor_scalar(kcT[lo:lo + 64].rearrange("p a n -> p (a n)"), b[lo:lo + 64, 30 * base:30 * base + 30],
                                      prm[lo:lo + 64, PRM["cmp_b2k"]:PRM["cmp_b2k"] + 1], None, ALU.add))
            steps.join()
            V.tensor_tensor(vc.rearrange("p (g d) -> p g d", g=4), b[0:NC, 64:320].rearrange("p (g d) -> p g d", g=4),
                            P("cmp_b2v", 0, 64, rows=NC).unsqueeze(1).broadcast_to([NC, 4, 64]), ALU.add)\
                .then_inc(freed[DVE_], 1)
            dve.wait_ge(freed[ACT_], TAKEN[GROUP0["nsagl"]])
            for n in range(2 * TT):
                t, base = divmod(n, 2)
                b = full("cmp_s", n)
                sv = b[:, 0:6 * NC].rearrange("p (h n) -> p h n", h=6)
                mx = cm[:, t, 6 * base:6 * base + 6]
                steps(V.tensor_reduce(mx, sv, X, ALU.max, negate=True))
                steps.join()
                V.tensor_tensor(cE[:, t, 90 * base:90 * base + 90].rearrange("p (h n) -> p h n", h=6), sv,
                                mx.unsqueeze(2).broadcast_to([128, 6, NC]), ALU.add).then_inc(c_e, 1)
                dve.drain().then_inc(freed[DVE_], 1)
            for t in range(TT):
                for base in range(2):
                    steps(V.tensor_copy(gcmp[:, t, 6 * base:6 * base + 6].rearrange("p (g r) -> p g r", g=2),
                                        ngl[:, t, :].rearrange("p (g b r k) -> p b g r k", g=2, b=2, r=3)[:, base, :, :, 0]))
            steps.join()
            for t in range(TT):
                dve.wait_ge(c_x, t + 1)
                ev = cE[:, t, :].rearrange("p (h n) -> p h n", h=12)
                steps(V.tensor_reduce(csum[:, t, :], ev, X, ALU.add))
                steps.join()
                steps(V.tensor_scalar(csum[:, t, :], csum[:, t, :], 1e-30, None, ALU.max))
                steps.join()
                steps(V.reciprocal(cr[:, t, :], csum[:, t, :]))
                steps.join()
                steps(V.scalar_tensor_tensor(out=cr[:, t, :], in0=cr[:, t, :],
                                             scalar=cst[:, CST["seen"] + t:CST["seen"] + t + 1],
                                             in1=gcmp[:, t, :],
                                             op0=ALU.mult, op1=ALU.mult))
                steps.join()
                V.tensor_tensor(ev, ev, cr[:, t, :].unsqueeze(2).broadcast_to([128, 12, NC]), ALU.mult).then_inc(c_p, 1)
            attend(JOBS1)
            attend(JOBS2)
            add_groups("wout1")
            norm("mean_f1", xT, [(hT, "norm_ffn", 8)])
            ffn("ffn1", 1)
            norm("mean_out", xT, [(hT, "final_norm", 0)])

        @block.tensor
        def _(pe):
            MM = nc.tensor.matmul

            def begin(stage, i=0):
                g = GROUP0[stage] + i
                if g >= 4:
                    pe.wait_ge(freed[TAKER[g - 4]], TAKEN[g - 4])
                return bank[g % 4]

            def slot(name, i):
                n = SLOT0[name] + i
                pe.wait_ge(w_full[n % RING], 16 * (n // RING + 1))
                return wring[:, n % RING, :]

            def mean(stage, src, before):
                b = begin(stage)
                for k in range(KT):
                    if k % 2 == 0:
                        pe.wait_ge(squared, before + k // 2 + 1)
                    ins = MM(b[:, 0:S], C("mean_d", 128), src[:, k, :], start=k == 0, stop=k == KT - 1)
                ins.then_inc(group_full, 1)

            def project(w, src, b, rows=128, tiles=2, kt=KT, width=None, norms=None):
                width = width or rows
                for m in range(tiles):
                    for k in range(kt):
                        if norms is not None and m == 0:
                            pe.wait_ge(normed, norms + k + 1)
                        ins = MM(b[0:rows, m * S:(m + 1) * S], w[:, (m * kt + k) * width:(m * kt + k) * width + rows],
                                 src[:, k, :], start=k == 0, stop=k == kt - 1)
                return ins

            def done(ins, stage=None):
                ins.then_inc(group_full, 1)

            pe.wait_ge(loaded, 32)
            pe.wait_ge(onehot_in, 16)
            for i in range(2):
                n = 512 if i == 0 else 384
                done(MM(begin("bias", i)[0:12, 0:n], P("rel", 0, 12, rows=33), onehots[:, 512 * i:512 * i + n], start=True, stop=True))
            mean("mean_x", sq, 0)
            for s in range(4):
                b = begin("win", s)
                done(project(slot("win", s), hT, b, norms=None if s else 0))
            with pe.Fori(1, 4) as i:
                for s in range(4):
                    g = GROUP0["win"] + s
                    if s < 4:
                        pe.wait_ge(freed[ACT_], i * 4 + (TAKEN[g] - 4))
                    n = SLOT0["win"] + s
                    pe.wait_ge(w_full[n % RING], (i + 1) * 16)
                    done(project(wring[:, n % RING, :], hT, bank[g % 4]))
            pe.wait_ge(pool_done, 1)
            for i in range(2):
                b = begin("poolmap", i)
                for j in range(2):
                    g = 2 * i + j
                    ins = MM(b[:, j * S:(j + 1) * S], P("group_w", 128 * g, 128), pooled[:, g, :], start=True, stop=True)
                done(ins)
            pe.wait_ge(conv_done, 1)
            pe.wait_ge(freed[ACT_], TAKEN[GROUP0["poolmap"] + 1])
            for i in range(4):
                w = slot("mix", i)
                for j in range(2):
                    m = 2 * i + j
                    b = begin("mix", m)
                    for br, src in enumerate((poolT, convT)):
                        for k in range(4):
                            o = ((j * 2 + br) * 4 + k) * 128
                            ins = MM(b[:, br * S:(br + 1) * S], w[:, o:o + 128], src[:, k, :], start=k == 0, stop=k == 3)
                    done(ins)
            pe.wait_ge(mixed, 8)
            for i in range(4):
                b = begin("wout", i)
                done(project(slot("wout", i), mT, b))
            mean("mean_ffn", sq, 8)
            mean("mean_mem", sqm, 4)
            pe.wait_ge(normed, 16)
            for t in range(TT):
                for k in range(KT):
                    ins = nc.tensor.transpose(wide[:, 2 * t + k // 4, (k % 4) * 128:(k % 4 + 1) * 128],
                                              hT[:, k, t * 128:(t + 1) * 128], ident)
            ins.then_inc(h2_ready, 1)

            def score(stage, i, c, t, w):
                b = begin(stage, i)
                for j in range(4):
                    hp = 4 * c + j
                    ins = MM(b[:, j * 128:(j + 1) * 128], qTa[:, hp, t * 128:(t + 1) * 128],
                             w[:, hp * 128:(hp + 1) * 128], start=True, stop=True)
                done(ins)

            for i in range(2):
                b = begin("wqa", i)
                done(project(slot("wqa", i), hT, b))
            w = slot("keysa", 0)
            pe.wait_ge(freed[ACT_], TAKEN[GROUP0["wqa"] + 1])
            score("scores_a", 0, 0, 0, w)
            pe.wait_ge(freed[DVE_], TAKEN[GROUP0["mean_mem"]])
            for i in range(6):
                b = begin("wq", i)
                done(project(slot("wq", i), hT, b))
            pe.wait_ge(freed[ACT_], TAKEN[GROUP0["wq"] + 5])
            w = slot("keys", 0)
            for i in range(7):
                t, c = divmod(i + 1, 4)
                score("scores", i, c, t, w)

            def memory():
                pe.wait_ge(normed, 32)
                for l in range(2):
                    b = begin("memkv", 2 * l)
                    done(project(slot("memkv", 2 * l), memn[l], b))
                    b = begin("memkv", 2 * l + 1)
                    w = slot("memkv", 2 * l + 1)
                    for t in range(TT):
                        for k in range(KT):
                            ins = MM(b[:, t * 256:(t + 1) * 256], memn[l][:, k, t * 128:(t + 1) * 128],
                                     w[:, k * 256:(k + 1) * 256], start=k == 0, stop=k == KT - 1)
                    done(ins)

            pe.wait_ge(freed[ACT_], TAKEN[GROUP0["scores"] + 6])
            pe.wait_ge(zeroed, 1)
            for t in range(TT):
                if t:
                    pe.wait_ge(peer_out, t)
                    memory()
                    pe.wait_ge(freed[ACT_], TAKEN[GROUP0["memkv"] + 3])
                for e in range(2):
                    MM(bank[e][:], zero[:, 0:128], zero[:], start=True, stop=False)
                with pe.Fori(t * HEADS // 2, (t + 1) * HEADS // 2) as i:
                    for s in range(2 * TOPK):
                        if s % 4 == 0:
                            pe.wait_ge(diags, i * 8 + (s // 4 + 1))
                        for e in range(2):
                            ins = MM(bank[e][:], diag[:, (s // 4) % 2, s % 4, :],
                                     G[:, s % NBUF, D + 512 * e:D + 512 * (e + 1)], start=False, stop=False)
                        ins.then_inc(v_used, 1)
                for e in range(2):
                    ins = MM(bank[e][:], zero[:, 0:128], zero[:], start=False, stop=True)
                ins.then_inc(peer_sum, 1)
            pe.wait_ge(peer_out, 2)
            for n in range(4):
                k4, t = divmod(n, 2)
                b = begin("peer_back", n)
                for k in range(4):
                    ins = nc.tensor.transpose(b[:, k * 128:(k + 1) * 128],
                                              peer_o[:, t, (4 * k4 + k) * 128:(4 * k4 + k + 1) * 128], ident)
                done(ins)
            mean("mean_fin", memn[0], 12)
            mean("mean_mix0", sqC, 16)
            for i in range(8):
                b = begin("gla_in", i)
                done(project(slot("gla96", i), hT, b, rows=DK, norms=None if i else 40))
            b = begin("gla_in", 8)
            done(project(slot("glamq", 0), hT, b))
            b = begin("gla_in", 9)
            done(project(slot("glalr", 0), hT, b, rows=16, tiles=1))
            for c in range(2):
                w = slot("glav", c)
                for t in range(TT):
                    b = begin("gla_in", 10 + 2 * c + t)
                    for k in range(KT):
                        ins = MM(b[:, 0:384], hT[:, k, t * 128:(t + 1) * 128], w[:, k * 384:(k + 1) * 384],
                                 start=k == 0, stop=k == KT - 1)
                    done(ins)
            for h in range(GH):
                if h % 2 == 0:
                    b = begin("gla_gate", h // 2)
                    pe.wait_ge(freed[ACT_], TAKEN[GROUP0["gla_in"] + 9])
                ins = MM(b[0:DK, (h % 2) * S:(h % 2 + 1) * S], P("w_gate_up", DK * h, DK, rows=16), glr, start=True, stop=True)
                if h % 2:
                    done(ins)
            for e in range(4):
                MM(wide[0:DK, e, :], zero[:, 0:DK], zero[:], start=True, stop=False)
            pe.wait_ge(freed[ACT_], TAKEN[GROUP0["gla_in"] + 13])

            def pair(level):
                last = level == LEVELS - 1
                if level:
                    pe.wait_ge(g_qk, level)
                kk, qq = (gk, gq) if level == 0 else (ke[(level - 1) % 2], qe[(level - 1) % 2])
                for t in range(1 if last else TT):
                    b = begin("gla_pair", 2 * level + t)
                    ti_ = 1 if last else t
                    for h in range(GH):
                        ins = MM(b[:, h * 128:(h + 1) * 128], kk[:, h, t * 128:(t + 1) * 128],
                                 qq[:, h, ti_ * 128:(ti_ + 1) * 128], start=True, stop=True)
                    done(ins)

            def give(level):
                last = level == LEVELS - 1
                for t in range(1 if last else TT):
                    g = 2 * level + t
                    ti_ = 1 if last else t
                    pe.wait_ge(freed[DVE_], TAKEN[GROUP0["gla_pair"] + g])
                    for h in range(GH):
                        for v in range(2):
                            o = (2 * h + v) * S + ti_ * 128
                            ins = MM(wide[0:DK, o // 512, o % 512:o % 512 + 128], gv[:, t, h * DV + v * DK:h * DV + (v + 1) * DK],
                                     pairs[:, g % 4, h, :], start=False, stop=False)
                    ins.then_inc(g_turn, 1)

            pair(0)
            for level in range(1, LEVELS):
                pair(level)
                give(level - 1)
            give(LEVELS - 1)
            for e in range(4):
                ins = MM(wide[0:DK, e, :], zero[:, 0:DK], zero[:], start=False, stop=True)
            ins.then_inc(g_done, 1)
            for h in range(GH):
                pe.wait_ge(g_sq, h // 2 + 1)
                if h % 2 == 0:
                    b = begin("gla_ms", h // 2)
                for v in range(2):
                    ins = MM(b[0:DK, (h % 2) * S:(h % 2 + 1) * S], C("mean_dv", DK, rows=DK), sqC[0:DK, 2 * h + v, :],
                             start=v == 0, stop=v == 1)
                if h % 2:
                    done(ins)

            def score(J):
                layer, kind, h, tt = JOBS[J]
                _, _, _, _, _, _, mq = job_bufs(layer)
                if J - 2 >= (0 if layer == 0 else JOBS1.start):
                    pe.wait_ge(a_m, J - 1)
                    pe.wait_ge(a_e, J - 1)
                cols = slice(tt * 128, tt * 128 + 128)
                for j in range(2):
                    if kind == "mem":
                        lo = 64 * (h % 2)
                        ins = MM(wide[:, J % 2, j * S:(j + 1) * S], mq[lo:lo + 64, h // 2, j * 128:(j + 1) * 128],
                                 memk[lo:lo + 64, layer, h // 2, :],
                                 start=True, stop=True)
                    else:
                        g, r = divmod(h, 3)
                        lo, w = 64 * (g % 2), 128 * (tt + 1)
                        ins = MM(wide[:, J % 2, j * S:j * S + w], nq[lo:lo + 64, (g // 2) * 3 + r, cols],
                                 ksw[lo:lo + 64, j, g // 2, 0:w], start=True, stop=True)
                ins.then_inc(a_s, 1)

            def turn(J):
                layer, kind, h, tt = JOBS[J]
                E = job_bufs(layer)[0]
                w = S if kind == "mem" else 128 * (tt + 1)
                pe.wait_ge(a_p, J + 1)
                if J:
                    pe.wait_ge(a_c, J)
                n = 0
                for j in range(2):
                    for k in range(w // 128):
                        ins = nc.tensor.transpose(wide[:, 2, n * 128:(n + 1) * 128], E[:, J % 2, j, k * 128:(k + 1) * 128], ident)
                        n += 1
                ins.then_inc(a_t, 1)

            def values(J):
                layer, kind, h, tt = JOBS[J]
                Pt = job_bufs(layer)[1]
                pe.wait_ge(a_c, J + 1)
                if J:
                    pe.wait_ge(a_done, J)
                if kind == "mem":
                    for j in range(2):
                        for k in range(TT):
                            ins = MM(wide[:, 3, j * 128:(j + 1) * 128], memv[:, layer, k, h // 2 * 128:(h // 2 + 1) * 128],
                                     Pt[:, J % 2, 2 * j + k, :], start=k == 0, stop=k == TT - 1)
                else:
                    g, r = divmod(h, 3)
                    gp = g // 2
                    MM(wide[:, 3, 0:128], vc[:, gp * 128:(gp + 1) * 128], pcT[:, tt, 6 * (g % 2) + 3 * gp + r, :], start=True, stop=False)
                    n = 0
                    for j in range(2):
                        for k in range(tt + 1):
                            ins = MM(wide[:, 3, 0:128], vsw[:, j, k, gp * 128:(gp + 1) * 128], Pt[:, J % 2, n, :],
                                     start=False, stop=n == 2 * tt + 1)
                            n += 1
                ins.then_inc(a_o, 1)

            def attend(jobs):
                score(jobs[0])
                score(jobs[1])
                for J in jobs:
                    turn(J)
                    if J + 2 in jobs:
                        score(J + 2)
                    values(J)

            pe.wait_ge(g_out, 1)
            attend(JOBS0)
            pe.wait_ge(a_done, JOBS0.stop)
            for i in range(4):
                b = begin("wout0", i)
                w = slot("wout0", i)
                for m in range(2):
                    for k in range(10):
                        rows = DK if k < 8 else 128
                        src = gout[:, k, :] if k < 8 else moT[:, k - 8, :]
                        o = (m * 10 + k) * 128
                        ins = MM(b[:, m * S:(m + 1) * S], w[0:rows, o:o + 128], src, start=k == 0, stop=k == 9)
                done(ins)

            def ffn(stage, layer, norms):
                g0, n0, k0 = GROUP0[stage], SLOT0[stage], layer * FT
                for n in range(4):
                    MM(wide[:, n, :], zero[:, 0:128], zero[:], start=True, stop=False)
                d0 = TAKEN[g0] - 1

                def up(j, k, norms=None):
                    pe.wait_ge(freed[DVE_], j + (d0 - 3))
                    n = n0 + k
                    if isinstance(j, int):
                        pe.wait_ge(w_full[n % RING], 16 * ((n0 + j) // RING + 1))
                    else:
                        pe.wait_ge(w_full[n % RING], up.i * 16 + 16 * (n // RING + 1))
                    done(project(wring[:, n % RING, :], hT, bank[(g0 + k) % 4], norms=norms))

                def down(j, k):
                    pe.wait_ge(f_hid, j + (k0 + 1))
                    w = wring[:, (n0 + k) % RING, :]
                    for m in range(KT):
                        ins = MM(wide[:, m // 2, (m % 2) * S:(m % 2 + 1) * S], w[:, (16 + m) * 128:(17 + m) * 128],
                                 fh[:, k % 2, :], start=False, stop=False)
                    ins.then_inc(f_down, 1)

                up(0, 0, norms)
                with pe.Fori(0, (FT - 2) // 4) as i:
                    up.i = i
                    for s in range(4):
                        up(i * 4 + (s + 1), s + 1)
                        down(i * 4 + s, s)
                up(FT - 1, FT - 1)
                down(FT - 2, FT - 2)
                down(FT - 1, FT - 1)
                for n in range(4):
                    ins = MM(wide[:, n, :], zero[:, 0:128], zero[:], start=False, stop=True)
                ins.then_inc(f_sum, 1)

            mean("mean_f0", sqF, 20)
            ffn("ffn0", 0, 48)
            mean("mean_kv", sqE, 24)
            pe.wait_ge(late, 80)
            for n in range(6):
                b = begin("flip", n)
                done(MM(b[:], C("flip", 128), hank[:, 2 * n:2 * n + 2, :].rearrange("p h t -> p (h t)"), start=True, stop=True))
            for i in range(4):
                b = begin("kv", i)
                done(project(slot("kv", i), hT, b, norms=None if i else 56))
            for i in range(4, 6):
                b = begin("kv", i)
                w = slot("kv", i)
                for t in range(TT):
                    for k in range(KT):
                        ins = MM(b[:, t * 256:(t + 1) * 256], hT[:, k, t * 128:(t + 1) * 128], w[:, k * 256:(k + 1) * 256],
                                 start=k == 0, stop=k == KT - 1)
                done(ins)
            for i in range(3):
                b = begin("nsaq", i)
                done(project(slot("nsaq", i), xn1, b, norms=None if i else 64))
            pe.wait_ge(c_pos, 8)
            pe.wait_ge(c_moved, 32)
            b = begin("cmp_hid")
            for kind in range(2):
                for l in range(LH):
                    ins = MM(b[:, 60 * kind:60 * kind + 60].rearrange("p (a n) -> p a n", a=2), w1[:, kind, l, :],
                             places[:, :, kind, l, :], start=l == 0, stop=l == LH - 1)
            done(ins)
            b = begin("nsamq")
            done(project(slot("nsamq", 0), xn1, b))
            b = begin("cmp_out")
            pe.wait_ge(freed[ACT_], TAKEN[GROUP0["cmp_hid"]])
            MM(b[:, 0:60], P("cmp_w2k", 0, 128), hid[:, 0, :], start=True, stop=True)
            for gp in range(2):
                for base in range(2):
                    o = 64 + (2 * gp + base) * 64
                    ins = MM(b[0:NC, o:o + 64], hid[:, 1, base * 30 + gp * NC:base * 30 + (gp + 1) * NC], P("cmp_w2v", 0, 64),
                             start=True, stop=True)
            done(ins)
            b = begin("nsagl")
            w = slot("nsagl", 0)
            for t in range(TT):
                for k in range(KT):
                    ins = MM(b[:, t * 36:(t + 1) * 36], xn1[:, k, t * 128:(t + 1) * 128], w[:, k * 36:(k + 1) * 36],
                             start=k == 0, stop=k == KT - 1)
            done(ins)
            pe.wait_ge(freed[DVE_], TAKEN[GROUP0["cmp_out"]])
            for n in range(2 * TT):
                t, base = divmod(n, 2)
                lo = 64 * base
                b = begin("cmp_s", n)
                for e in range(6):
                    gp, r = divmod(e, 3)
                    MM(b[:, e * NC:(e + 1) * NC], nq[lo:lo + 64, gp * 3 + r, t * 128:(t + 1) * 128],
                       kcT[lo:lo + 64, gp, :], start=True, stop=False)
                    ins = MM(b[:, e * NC:(e + 1) * NC], biasC[:, (2 * gp + base) * 3 + r, t * 128:(t + 1) * 128],
                             cst[0:NC, CST["flip"] + 128 - NC:CST["flip"] + 128], start=False, stop=True)
                done(ins)
            pe.wait_ge(freed[ACT_], TAKEN[GROUP0["nsagl"]])
            attend(JOBS1)
            for n in range(6):
                t, c = divmod(n, 3)
                b = begin("cmp_pT", n)
                pe.wait_ge(c_p, t + 1)
                for j in range(4):
                    h = 4 * c + j
                    ins = nc.tensor.transpose(b[0:NC, j * 128:(j + 1) * 128], cE[:, t, h * NC:(h + 1) * NC], ident)
                done(ins)
            pe.wait_ge(freed[ACT_], TAKEN[GROUP0["cmp_pT"] + 5])
            attend(JOBS2)
            pe.wait_ge(a_done, JOBS2.stop)
            for i in range(4):
                b = begin("wout1", i)
                w = slot("wout1", i)
                for m in range(2):
                    for k in range(KT):
                        src = naT[:, k, :] if k < 6 else moT1[:, k - 6, :]
                        o = (m * KT + k) * 128
                        ins = MM(b[:, m * S:(m + 1) * S], w[:, o:o + 128], src, start=k == 0, stop=k == KT - 1)
                done(ins)
            mean("mean_f1", sqF, 28)
            ffn("ffn1", 1, 72)
            mean("mean_out", sqF, 32)


def pack(w, width=128):
    kt, nt = w.shape[0] // 128, w.shape[1] // width
    t = w.reshape(kt, 128, nt, width).transpose(2, 1, 0, 3).reshape(nt // 2, 2, 128, kt * width)
    return t.transpose(0, 2, 1, 3).reshape(nt // 2, 128, 2 * kt * width)


def moving(w):
    return w.reshape(w.shape[0] // 128, 128, -1).transpose(1, 0, 2).reshape(1, 128, -1)


def layout(i):
    import numpy as np

    f = np.float32
    cat = np.concatenate
    col = lambda v: v.reshape(-1, 128).T
    L = {}
    L["xT"] = i["x"][0].T.reshape(KT, 128, S).transpose(1, 0, 2)
    L["memT"] = i["mem_2"][0].T.reshape(KT, 128, S).transpose(1, 0, 2)
    L["win"] = pack(i["w_in"][0])
    br = np.stack([w.reshape(4, 128, KT, 128).transpose(2, 1, 0, 3) for w in (i["w_branch_pool"][0], i["w_branch_conv"][0])], 2)
    L["mix"] = br.reshape(4, 2, 128, 1024).transpose(0, 2, 1, 3).reshape(4, 128, 2048)
    L["wout"] = pack(i["w_out"][0])
    wq = pack(i["w_q"][0])
    L["wqa"], L["wq"] = wq[0:2], wq[2:8]
    L["keys"] = i["sub_keys"][0].transpose(3, 0, 1, 2).reshape(1, 128, 2048)
    mk = i["w_mem_kv_2"]
    L["keysa"] = L["keys"][:, :, 0:512]
    L["memkv"] = cat([x for l in range(2) for x in (pack(mk[l][:, 0:256]), moving(mk[l][:, 256:512]))])
    gw = i["gla_w_in_2"][0]
    L["gla96"] = pack(cat([gw[:, 0:768], gw[:, 1536:2304]], 1), DK)
    L["glamq"] = pack(gw[:, 2320:2576])
    L["glalr"] = moving(gw[:, 2304:2320])
    L["glav"] = cat([moving(gw[:, 768:1152]), moving(gw[:, 1152:1536])])
    wo = i["w_out_2"]
    rows = np.zeros((10, 128, D), f)
    rows[0:8, 0:DK] = wo[0][0:768].reshape(8, DK, D)
    rows[8:10] = wo[0][768:].reshape(2, 128, D)
    L["wout0"] = pack(rows.reshape(1280, D))
    for l in range(2):
        up, down = i["w_up_2"][l], i["w_down_2"][l]
        ab = up.reshape(KT, 128, 2, FT, 128).transpose(3, 1, 2, 0, 4).reshape(FT, 128, 2048)
        L[f"ffn{l}"] = cat([ab, down.reshape(FT, 128, D)], 2)
    kv = i["w_kv_shared_2"].reshape(D, 6, 256)
    L["kv"] = cat([pack(kv[:, n]) for n in (0, 1, 2, 4)] + [moving(kv[:, n]) for n in (3, 5)])
    nw = i["nsa_w_in_2"][0]
    perm = lambda w: w.reshape(2, 2, 3, 64, -1).transpose(0, 2, 1, 3, 4).reshape(768, -1)
    L["nsaq"] = pack(np.ascontiguousarray(perm(nw[:, 0:768].T).T))
    L["nsamq"] = pack(nw[:, 804:1060])
    L["nsagl"] = moving(nw[:, 768:804])
    L["wout1"] = pack(cat([perm(wo[1][0:768]), wo[1][768:]]))
    L["uv"] = cat([i["expert_u"][0], i["expert_v"][0]], 1)
    L["w1"] = i["cmp_w1_2"].reshape(2, 2, 16, 64, 128).transpose(1, 3, 0, 2, 4).reshape(128, 2, 16, 128)
    p = np.zeros((128, PRM_W), f)

    def put(name, v):
        p[0:v.shape[0], PRM[name]:PRM[name] + v.shape[1]] = v

    put("g_mix", col(i["g_mix"][0]))
    put("g_ffn", col(i["g_ffn"][0]))
    put("g_final", col(i["g_final"]))
    put("norm_mix", col(i["norm_mix_2"]))
    put("norm_mem", col(i["norm_mem_2"]))
    put("norm_ffn", col(i["norm_ffn_2"]))
    put("kv_norm", col(i["kv_norm_2"]))
    put("final_norm", col(i["final_norm_2"]))
    put("pool_scale", col(i["pool_scale"][0]))
    put("conv_w", i["conv_w"][0].reshape(3, 4, 128).transpose(2, 1, 0).reshape(128, 12))
    put("ffn_w", i["conv_w_2"].reshape(2, 3, 2 * FT, 128).transpose(3, 0, 2, 1).reshape(128, -1))
    put("ffn_b", i["conv_b_2"].reshape(2 * 2 * FT, 128).T)
    put("b_gate", i["gla_b_gate_2"][0].reshape(GH, DK).T)
    put("out_norm", i["gla_out_norm_2"][0].reshape(2, DK).T)
    put("cmp_b1", i["cmp_b1_2"].T)
    put("cmp_b2k", np.tile(i["cmp_b2_2"][0], 2)[:, None])
    put("cmp_b2v", np.tile(i["cmp_b2_2"][1][None], (NC, 1)))
    put("group_w", i["pool_group_w"][0].transpose(1, 0, 2).reshape(128, 512))
    put("cmp_w2k", np.tile(i["cmp_w2_2"][0], (1, 2)))
    put("cmp_w2v", i["cmp_w2_2"][1])
    put("w_gate_up", i["gla_w_gate_up_2"][0])
    put("cmp_pos", np.tile(i["cmp_pos_2"].transpose(2, 0, 1).reshape(64, 64), (2, 1)))
    put("rel", cat([i["rel_bias_2"], np.ones((1, 12), f)]))
    L["prm"] = p
    c = np.zeros((128, CST_W), f)
    r = np.arange(128)
    c[r, CST["ident"] + r] = 1
    c[r, CST["flip"] + 127 - r] = 1
    c[:, CST["mean_d"]:CST["mean_d"] + 128] = 1.0 / D
    c[:, CST["mean_dv"]:CST["mean_dv"] + 128] = 1.0 / DV
    c[:, CST["iota"]:CST["iota"] + 16] = np.arange(16)
    c[31:, CST["seen"]] = 1
    c[:, CST["seen"] + 1] = 1
    L["cst"] = c
    t = np.arange(S)
    L["invcnt"] = np.tile(np.stack([1.0 / np.minimum(t + 1, w) for w in (2, 4, 8, 16)]).astype(f)[None], (128, 1, 1))
    L["reset"] = np.tile(np.stack([np.arange(GH * S) % n != 0 for n in (16, S)]).astype(f)[None], (DK, 1, 1))
    half = lambda n: r // (1 << n)
    L["lvmask"] = np.stack([((half(n)[:, None] % 2 == 0) & (half(n)[:, None] + 1 == half(n)[None, :])) for n in
                            range(LEVELS - 2)], 1).astype(f)
    dist = cat([np.arange(512) - 255, 255 - np.arange(384)])
    far = 16 + (np.log(np.maximum(dist, 1) / 16.0) / np.log(8.0) * 16 + 1e-9).astype(np.int64)
    bucket = np.where(dist < 16, dist, np.minimum(far, 31))
    oh = np.zeros((33, 896), f)
    n = np.arange(896)
    oh[bucket[dist >= 0], n[dist >= 0]] = 1
    oh[32, dist < 0] = -1e30
    L["onehot"] = oh
    return {k: np.ascontiguousarray(v) for k, v in L.items()}


def kernel(**inputs):
    import numpy as np
    import concourse.bacc as bacc
    from concourse.bass_utils import run_bass_kernel_spmd

    nc = bacc.Bacc("TRN2", target_bir_lowering=False, num_devices=1)
    arrays = layout({k: np.asarray(v) for k, v in inputs.items()})
    f32 = mybir.dt.float32
    a = {k: nc.dram_tensor(k + "_dram", v.shape, f32, kind="ExternalInput").ap() for k, v in arrays.items()}
    a["rows"] = nc.dram_tensor("rows_dram", (12, 896), f32, kind="Internal").ap()
    out = nc.dram_tensor("out_dram", (128, KT, S), f32, kind="ExternalOutput").ap()
    program(nc, a, out)
    r = run_bass_kernel_spmd(nc, [{k + "_dram": v for k, v in arrays.items()}], core_ids=[0])
    y = r.results[0]["out_dram"]
    return np.ascontiguousarray(y.transpose(2, 1, 0)).reshape(1, S, D)
```
